# Optimizing a Trainium2 kernel written in Bass

```python
import jax, jax.numpy as jnp
from jax import lax
import numpy as np

D_MODEL = 1024
BATCH = 1
SEQ = 256
DEPTH = 2

CHUNK = 64
N_META = 16
POOL_WINDOWS = (2, 4, 8, 16)
N_POOL_GROUPS = len(POOL_WINDOWS)
POOL_GROUP = D_MODEL // N_POOL_GROUPS
CONV_WIDTH = 3
D_FF = 7 * D_MODEL // 2
N_EXPERTS = 8
TOP_K = 2
EPS = 1e-6
N_POOL_LAYERS = (DEPTH + 1) // 2
N_CONV_LAYERS = DEPTH // 2

kernel_name = "hybrid_pool_shortconv_moe_encoder"

def rms_norm(x, g):
    xf = x.astype(jnp.float32)
    y = xf * lax.rsqrt(jnp.mean(xf * xf, axis=-1, keepdims=True) + EPS)
    return (y * g.astype(jnp.float32)).astype(x.dtype)

def pool_mixer(h, w_grp, scale):
    T = h.shape[1]
    hf = h.astype(jnp.float32)
    cs = jnp.cumsum(hf, axis=1)
    pos = jnp.arange(1, T + 1, dtype=jnp.float32)[:, None]
    outs = []
    for g, w in enumerate(POOL_WINDOWS):
        sl = slice(g * POOL_GROUP, (g + 1) * POOL_GROUP)
        c = cs[..., sl]
        lower = jnp.pad(c, ((0, 0), (w, 0), (0, 0)))[:, :T]
        mean = (c - lower) / jnp.minimum(pos, float(w))
        d = (mean - hf[..., sl]).astype(h.dtype)
        outs.append(jnp.einsum('btc,cd->btd', d, w_grp[g]))
    return jnp.concatenate(outs, axis=-1) * scale

def conv_mixer(h, w_in, conv_k, w_out):
    bcv = jnp.einsum('btd,de->bte', h, w_in)
    b, c, v = jnp.split(bcv, 3, axis=-1)
    u = c * v
    y = lax.conv_general_dilated(
        u, conv_k[:, None, :], window_strides=(1,), padding=[(CONV_WIDTH - 1, 0)],
        dimension_numbers=('NWC', 'WIO', 'NWC'), feature_group_count=u.shape[-1])
    return jnp.einsum('btd,de->bte', b * y, w_out)

def swiglu(h, w_gate, w_up, w_down):
    a = jnp.einsum('btd,df->btf', h, w_gate)
    u = jnp.einsum('btd,df->btf', h, w_up)
    return jnp.einsum('btf,fd->btd', jax.nn.silu(a) * u, w_down)

def moe_swiglu(h, router, w_gate, w_up, w_down):
    logits = jnp.einsum('btd,de->bte', h, router).astype(jnp.float32)
    top_v, top_i = lax.top_k(logits, TOP_K)
    top_w = jax.nn.softmax(top_v, axis=-1)
    gates = jnp.sum(jax.nn.one_hot(top_i, N_EXPERTS, dtype=jnp.float32) * top_w[..., None], axis=-2)
    gates = gates.astype(h.dtype)
    out = jnp.zeros_like(h)
    for e in range(N_EXPERTS):
        out = out + gates[..., e:e + 1] * swiglu(h, w_gate[e], w_up[e], w_down[e])
    return out

def setup_inputs(seed: int = 0) -> dict:
    key = jax.random.key(seed)
    ks = jax.random.split(key, 20)
    D, F, E, G, Dg = D_MODEL, D_FF, N_EXPERTS, N_POOL_GROUPS, POOL_GROUP
    Lp, Lc = N_POOL_LAYERS, N_CONV_LAYERS
    nrm = lambda k, s, sc: jax.random.normal(k, s, jnp.float32) * sc
    gain = lambda k, s: 1.0 + 0.05 * jax.random.normal(k, s, jnp.float32)
    return {
        "x": nrm(ks[0], (BATCH, SEQ, D), 1.0),
        "meta_tokens": nrm(ks[1], (N_META, D), 1.0),
        "pool_norm": gain(ks[2], (Lp, D)),
        "pool_w": nrm(ks[3], (Lp, G, Dg, Dg), Dg ** -0.5),
        "pool_scale": gain(ks[4], (Lp, D)),
        "dense_norm": gain(ks[5], (Lp, D)),
        "dense_w_gate": nrm(ks[6], (Lp, D, F), D ** -0.5),
        "dense_w_up": nrm(ks[7], (Lp, D, F), D ** -0.5),
        "dense_w_down": nrm(ks[8], (Lp, F, D), F ** -0.5),
        "conv_norm": gain(ks[9], (Lc, D)),
        "conv_w_in": nrm(ks[10], (Lc, D, 3 * D), D ** -0.5),
        "conv_kernel": nrm(ks[11], (Lc, CONV_WIDTH, D), CONV_WIDTH ** -0.5),
        "conv_w_out": nrm(ks[12], (Lc, D, D), D ** -0.5),
        "moe_norm": gain(ks[13], (Lc, D)),
        "moe_router": nrm(ks[14], (Lc, D, E), D ** -0.5),
        "moe_w_gate": nrm(ks[15], (Lc, E, D, F), D ** -0.5),
        "moe_w_up": nrm(ks[16], (Lc, E, D, F), D ** -0.5),
        "moe_w_down": nrm(ks[17], (Lc, E, F, D), F ** -0.5),
        "final_norm": gain(ks[18], (D,)),
    }

def reference(x, meta_tokens, pool_norm, pool_w, pool_scale, dense_norm, dense_w_gate, dense_w_up,
              dense_w_down, conv_norm, conv_w_in, conv_kernel, conv_w_out, moe_norm, moe_router,
              moe_w_gate, moe_w_up, moe_w_down, final_norm):
    B = x.shape[0]
    meta = jnp.broadcast_to(meta_tokens[None].astype(x.dtype), (B, N_META, x.shape[-1]))
    h = jnp.concatenate([meta, x], axis=1)
    for i in range(DEPTH):
        j = i // 2
        if i % 2 == 0:
            h = h + pool_mixer(rms_norm(h, pool_norm[j]), pool_w[j], pool_scale[j])
            h = h + swiglu(rms_norm(h, dense_norm[j]), dense_w_gate[j], dense_w_up[j], dense_w_down[j])
        else:
            h = h + conv_mixer(rms_norm(h, conv_norm[j]), conv_w_in[j], conv_kernel[j], conv_w_out[j])
            h = h + moe_swiglu(rms_norm(h, moe_norm[j]), moe_router[j], moe_w_gate[j], moe_w_up[j],
                               moe_w_down[j])
    out = rms_norm(h, final_norm)
    return out[:, N_META:]


_drawn_inputs = setup_inputs


def setup_inputs(seed=0):
    import zlib

    import numpy as np

    out = dict(_drawn_inputs(seed))
    spreads = {}
    factors = {}
    for name, (base, spread) in spreads.items():
        noise = np.random.default_rng([zlib.crc32(name.encode()), seed]).standard_normal(out[name].shape)
        drawn = base * np.exp(spread * noise) if base else spread * noise
        out[name] = __import__('jax').numpy.asarray(drawn.astype(out[name].dtype))
    for name, factor in factors.items():
        out[name] = (out[name] * factor).astype(out[name].dtype)
    return out
```

```python
from contextlib import ExitStack

import concourse.bass as bass
from concourse import mybir

ACT = mybir.ActivationFunctionType
ALU = mybir.AluOpType
AX_X = mybir.AxisListType.X
F32 = mybir.dt.float32
F32R = mybir.dt.float32r
I32 = mybir.dt.int32
U32 = mybir.dt.uint32

P = 128


def build_encoder(nc, x, meta_tokens, pool_norm, pool_w, pool_scale, dense_norm, dense_w_gate,
                  dense_w_up, dense_w_down, conv_norm, conv_w_in, conv_kernel, conv_w_out,
                  moe_norm, moe_router, moe_w_gate, moe_w_up, moe_w_down, final_norm, out):
    SEQ, D = x.shape[1], x.shape[2]
    N_META = meta_tokens.shape[0]
    T = SEQ + N_META
    F = dense_w_gate.shape[2]
    E = moe_router.shape[2]
    TAPS = conv_kernel.shape[1]
    GROUPS, GW = pool_w.shape[1], pool_w.shape[2]
    WINDOWS = (2, 4, 8, 16)
    EPS = 1e-6
    KD = D // P
    KF = F // P
    NS = SEQ + TAPS - 1
    OLD = T - NS
    TT = SEQ // P
    STEPS = F // 512
    assert (KD, TT, GW, GROUPS, E, KF, STEPS, TAPS) == (8, 2, 256, 4, 8, 28, 7, 3)

    RING = 7
    GRAN, SUB = 2048, 1024
    G_GU = 1
    G_DN = G_GU + 2 * KF // 2
    G_CI = G_DN + KF // 2
    G_CO = G_CI + 3 * D // 256
    G_MOE = G_CO + D // 256
    PASS_G = 6 * STEPS
    PASS_S = 2 * PASS_G
    Q_MOE = 2 * G_MOE
    LEAD = 4
    assert PASS_G % RING == 0 and (4 * KF // 4) % RING == 0

    with ExitStack() as ctx:
        def sem(name):
            return ctx.enter_context(nc.semaphore(name))

        base = (nc.sbuf_base + 63) // 64 * 64
        at = [base]

        def region(nbytes):
            a = at[0]
            at[0] += (nbytes + 31) // 32 * 32
            return a

        def place(name, addr, shape, dt):
            return nc.alloc_sbuf_tensor_at(name, shape, dt, offset=addr)

        A_RAW, A_HI, A_LO = region(RING * GRAN * 4), region(RING * SUB * 4), region(RING * SUB * 4)
        A_AH, A_AL = region(KF * NS * 4), region(KF * NS * 4)
        A_NH, A_NL = region(KD * NS * 4), region(KD * NS * 4)
        A_XN, A_X = region(KD * T * 4), region(KD * T * 4)

        raw = place("raw", A_RAW, [P, RING, GRAN], F32)
        w_hi = place("w_hi", A_HI, [P, RING, SUB], F32R)
        w_lo = place("w_lo", A_LO, [P, RING, SUB], F32R)
        X = place("X", A_X, [P, KD, T], F32)
        xn = place("xn", A_XN, [P, KD * T], F32)
        n_hi = place("n_hi", A_NH, [P, KD, NS], F32R)
        n_lo = place("n_lo", A_NL, [P, KD, NS], F32R)
        hid_hi = place("hid_hi", A_AH, [P, KF, NS], F32R)
        hid_lo = place("hid_lo", A_AL, [P, KF, NS], F32R)
        param_rows = place("param_rows", A_AL, [64, P], F32)
        tok = place("tok", A_RAW + 5 * GRAN * 4, [P, 3, D], F32)
        hp = place("hp", A_RAW + 5 * GRAN * 4 + 3 * D * 4, [P, 1 + T], F32)
        sa = place("sa", A_RAW + 5 * GRAN * 4 + 3 * D * 4 + 1152, [P, 1 + T], F32)
        sb = place("sb", A_RAW + 5 * GRAN * 4 + 3 * D * 4 + 2304, [P, 1 + T], F32)
        hn_hi = place("hn_hi", A_AH, [P, TT, D], F32R)
        hn_lo = place("hn_lo", A_AL, [P, TT, D], F32R)
        xg_hi = place("xg_hi", A_AH + 8192, [P, KD, P], F32R)
        xg_lo = place("xg_lo", A_AL + 8192, [P, KD, P], F32R)
        mT_hi = place("mT_hi", A_AH + 12288, [P, 4, P], F32R)
        mT_lo = place("mT_lo", A_AL + 12288, [P, 4, P], F32R)
        y_hi = place("y_hi", A_AH + 14336, [P, D], F32R)
        y_lo = place("y_lo", A_AL + 14336, [P, D], F32R)
        pick = place("pick", A_AH + 18432, [P, TT, P], F32R)
        pickT = place("pickT", A_AH + 19456, [P, TT, P], F32R)
        racc = place("racc", A_XN, [P, TT, D], F32)
        gfin = place("gfin", A_NH, [P, D], F32)
        silu_m = place("silu_m", A_NL, [P, 512], F32)
        hid_m = place("hid_m", A_NL + 2048, [P, 512], F32)
        junk = place("junk", A_X, [P, D], F32)

        ident = place("ident", region(512), [P, P], F32)
        ones = place("ones", region(512), [P, P], F32)
        before = place("before", region(512), [P, P], F32)
        iota = place("iota", region(512), [P, P], F32)
        prm = place("prm", region(256), [P, 64], F32)
        r32 = place("r32", region(256), [P, KD, E], F32)
        r_hi = place("r_hi", region(256), [P, KD, E], F32R)
        r_lo = place("r_lo", region(256), [P, KD, E], F32R)
        lg = place("lg", region(64), [P, TT, E], F32)
        mx = place("mx", region(64), [P, TT, E], F32)
        ix = place("ix", region(64), [P, TT, E], U32)
        ixf = place("ixf", region(64), [P, TT, E], F32)
        oh1 = place("oh1", region(64), [P, TT, E], F32)
        oh2 = place("oh2", region(64), [P, TT, E], F32)
        mask = place("mask", region(64), [P, TT, E], F32)
        gates = place("gates", region(64), [P, TT, E], F32)
        slot_of = place("slot_of", region(160), [P, TT, 20], F32)
        rank = place("rank", region(64), [P, TT, E], F32)
        gw = place("gw", region(64), [P, 4, TT], F32)
        small = place("small", region(64), [P, 16], F32)
        npass = place("npass", region(32), [P, 1], I32)
        assert at[0] <= nc.sbuf_usable_end, at[0] - nc.sbuf_usable_end
        eps, cmax, ssum, rstd, slot_gate = (small[:, 0:1], small[:, 1:2], small[:, 2:4],
                                            small[:, 4:6], small[:, 6:7])
        ps = ctx.enter_context(nc.psum_tensor("ps", [P, 8, 512], F32))

        PN, PS, DN, CN, MN, CK = 0, KD, 2 * KD, 3 * KD, 4 * KD, 5 * KD

        tok_in, prm_in, rout_in, gfin_in, out_done = (sem("tok_in"), sem("prm_in"), sem("rout_in"),
                                                      sem("gfin_in"), sem("out_done"))
        raw_full = [sem(f"raw_full{i}") for i in range(RING)]
        hi_done, lo_done, sub_done = sem("hi_done"), sem("lo_done"), sem("sub_done")
        consts, xT_ready, x_act, x_dve = sem("consts"), sem("xT_ready"), sem("x_act"), sem("x_dve")
        dve_step = sem("dve_step")
        sq_done, ss_ready, rt_done, xn_done = sem("sq_done"), sem("ss_ready"), sem("rt_done"), sem("xn_done")
        nh_done, nl_done, x_new = sem("nh_done"), sem("nl_done"), sem("x_new")
        dn_ready, co_ready = sem("dn_ready"), sem("co_ready")
        dsilu, dmul, dhid_hi, dhid_lo = sem("dsilu"), sem("dmul"), sem("dhid_hi"), sem("dhid_lo")
        c_copied, u_made, z_made, z_hi_done, z_lo_done = (
            sem("c_copied"), sem("u_made"), sem("z_made"), sem("z_hi_done"), sem("z_lo_done"))
        arena_zero, rT_ready, racc_done, hnT_ready, hn_hi_done, hn_lo_done = (
            sem("arena_zero"), sem("rT_ready"), sem("racc_done"), sem("hnT_ready"), sem("hn_hi_done"), sem("hn_lo_done"))
        rh_done, rl_done, lg_ready, mask_done, pos_ready, dlog, elog, route_done = (
            sem("rh_done"), sem("rl_done"), sem("lg_ready"), sem("mask_done"), sem("pos_ready"), sem("dlog"),
            sem("elog"), sem("route_done"))
        t_ready, y_zero, gath_ready, comb_ready, pt_ready = (
            sem("t_ready"), sem("y_zero"), sem("gath_ready"),
            sem("comb_ready"), sem("pt_ready"))
        silu_done, mul_done, mTh_done, mTl_done, yh_done, yl_done = (
            sem("silu_done"), sem("mul_done"), sem("mTh_done"), sem("mTl_done"), sem("yh_done"), sem("yl_done"))
        xgh_done, xgl_done, pT_done, gs_done, pick_done, comb_added = (
            sem("xgh_done"), sem("xgl_done"), sem("pT_done"), sem("gs_done"), sem("pick_done"), sem("comb_added"))
        ss_fin, rt_fin, o_done = sem("ss_fin"), sem("rt_fin"), sem("o_done")

        def raw_slot(g):
            return g % RING

        def up_step(s):
            return 0 if s == 0 else 12 * s - 4

        def up_end(s):
            return up_step(s) + 7

        def turn_after(s):
            return 12 * s + 11 if s < STEPS - 1 else PASS_S - 5

        block = ctx.enter_context(nc.Block())

        @block.sync
        def _(sp):
            sp.dma_start(tok[0:N_META, 0, :], meta_tokens).then_inc(tok_in, 16)
            sp.dma_start(tok[N_META:P, 0, :], x[0, 0:P - N_META, :]).then_inc(tok_in, 16)
            sp.dma_start(tok[:, 1, :], x[0, P - N_META:2 * P - N_META, :]).then_inc(tok_in, 16)
            sp.dma_start(tok[0:T - 2 * P, 2, :], x[0, 2 * P - N_META:SEQ, :]).then_inc(tok_in, 16)

            def load(g, turns, src, dst_pat, **sizes):
                if g >= RING or not isinstance(turns, int):
                    sp.wait_ge(lo_done, 2 * (g - RING) + 2 + 2 * RING * turns)
                s = raw_slot(g)
                dst = raw[:, s, :].rearrange(dst_pat, **sizes)
                sp.dma_start(dst, src).then_inc(raw_full[s], 16)

            load(0, 0, pool_w[0].rearrange("g (k p) f -> p (g k) f", p=P), "p (a f) -> p a f", f=GW)
            def gate_up(g, turns, col):
                for w in (dense_w_gate, dense_w_up):
                    if g == RING - 2 or g == RING - 1:
                        sp.wait_ge(nl_done, KD)
                    load(g, turns, w[0][:, col].rearrange("(k p) f -> p k f", p=P),
                         "p (k f) -> p k f", k=KD)
                    g += 1
            for n in range(STEPS):
                gate_up(G_GU + 2 * n, 0, slice(256 * n, 256 * n + 256))
            with sp.Fori(1, 2) as it:
                for n in range(STEPS):
                    gate_up(G_GU + 2 * n + 2 * RING, (it - 1) * 2,
                            bass.ds(256 * STEPS * it + 256 * n, 256))
            for n in range(2 * STEPS):
                half, i = divmod(n, STEPS)
                load(G_DN + n, 0, dense_w_down[0, 512 * i:512 * i + 512, 512 * half:512 * half + 512]
                     .rearrange("(k p) f -> p k f", p=P), "p (k f) -> p k f", k=4)
            for n in range(3 * KD // 2):
                j, part = divmod(n, 3)
                col = (1, 2, 0)[part] * D + 256 * j
                load(G_CI + n, 0, conv_w_in[0, :, col:col + 256].rearrange("(k p) f -> p k f", p=P),
                     "p (k f) -> p k f", k=KD)
            for n in range(KD // 2):
                load(G_CO + n, 0, conv_w_out[0, :, 256 * n:256 * n + 256].rearrange("(k p) f -> p k f", p=P),
                     "p (k f) -> p k f", k=KD)

            def expert(t):
                e = t % E
                g = G_MOE

                def turns():
                    return t * (PASS_G // RING)

                def up_like(g, w, s):
                    for h in range(2):
                        load(g + h, turns(), w[0][bass.ds(e, 1), 512 * h:512 * h + 512, 512 * s:512 * s + 512]
                             .rearrange("a (k p) f -> p (a k) f", p=P), "p (k f) -> p k f", k=4)

                def down(g, s):
                    for h in range(2):
                        r = 512 * s + 256 * h
                        load(g + h, turns(), moe_w_down[0][bass.ds(e, 1), r:r + 256, :]
                             .rearrange("a (k p) f -> p (a k) f", p=P), "p (k f) -> p k f", k=2)

                for s in range(STEPS):
                    up_like(g, moe_w_gate, s)
                    up_like(g + 2, moe_w_up, s)
                    g += 4
                    if s >= 1:
                        down(g, s - 1)
                        g += 2
                down(g, STEPS - 1)

            expert(0)
            sp.wait_ge(route_done, 1)
            n_pass = sp.value_load(npass[0:1, 0:1], min_val=E, max_val=2 * E)
            with sp.Fori(1, n_pass) as t:
                expert(t)
            for tt in range(TT):
                sp.wait_ge(o_done, tt + 1)
                sp.dma_start(out[0, tt * P:(tt + 1) * P, :], racc[:, tt, :]).then_inc(out_done, 16)
            sp.wait_ge(out_done, 16 * TT)

        @block.gpsimd
        def _(pool):
            pool.memset(ones[:, :], 1.0).then_inc(consts, 1)
            pool.memset(ident[:, :], 0.0).then_inc(consts, 1)
            pool.memset(eps, EPS).then_inc(consts, 1)
            pool.memset(hp[:, 0:1], 0.0).then_inc(consts, 1)
            pool.iota(iota[:, :], pattern=[[1, P]], base=0, channel_multiplier=0,
                      allow_small_or_imprecise_dtypes=True).then_inc(consts, 1)
            pool.memset(slot_of[:, :, :], -1.0).then_inc(consts, 1)
            pool.wait_ge(consts, 6)
            pool.affine_select(out=ident[:, :], in_=ident[:, :], compare_op=ALU.not_equal, fill=1.0,
                               base=0, pattern=[[-1, P]], channel_multiplier=1).then_inc(consts, 1)
            pool.affine_select(out=before[:, :], in_=ones[:, :], compare_op=ALU.is_gt, fill=0.0,
                               base=0, pattern=[[1, P]], channel_multiplier=-1).then_inc(consts, 1)
            pool.wait_ge(sub_done, Q_MOE)
            pool.memset(y_hi[:, :].bitcast(F32), 0.0).then_inc(arena_zero, 1)
            pool.memset(y_lo[:, :].bitcast(F32), 0.0).then_inc(arena_zero, 1)
            pool.memset(pickT[:, :, :].bitcast(F32), 0.0).then_inc(arena_zero, 1)
            pool.memset(slot_gate, 0.0).then_inc(arena_zero, 1)

        @block.scalar
        def _(act):
            act.sem_inc(silu_done, 1)
            act.sem_inc(pT_done, 1)
            prm_src = [(pool_norm, 1), (pool_scale, 1), (dense_norm, 1), (conv_norm, 1), (moe_norm, 1)]
            row = 0
            for src, _ in prm_src:
                act.dma_start(param_rows[row:row + KD, :], src[0].rearrange("(c p) -> c p", p=P)).then_inc(prm_in, 16)
                row += KD
            act.dma_start(param_rows[row:row + TAPS * KD, :],
                          conv_kernel[0].rearrange("t (c p) -> (t c) p", p=P)).then_inc(prm_in, 16)
            act.dma_start(r32[:, :, :], moe_router[0].rearrange("(k p) e -> p k e", p=P)).then_inc(rout_in, 16)

            def hi(q, turns=0):
                if q % 2 == 0:
                    g = q // 2
                    act.wait_ge(raw_full[raw_slot(g)], 16 * (g // RING + 1) + 16 * turns)
                if q >= RING:
                    act.wait_ge(sub_done, q - RING + 1 + 2 * RING * turns)
                nc.scalar.activation(w_hi[:, q % RING, :],
                                     raw[:, raw_slot(q // 2), (q % 2) * SUB:(q % 2 + 1) * SUB],
                                     ACT.Copy).then_inc(hi_done, 1)

            def squares(nn, col, n, chunks=range(KD)):
                for c in chunks:
                    act.wait_ge(x_new, KD * (nn - 1) + c + 1)
                    nc.scalar.activation(xn[:, c * T:c * T + n], X[:, c, col:col + n], ACT.Square).then_inc(sq_done, 1)

            def root(nn, bank, n):
                act.wait_ge(ss_ready, nn + 1)
                nc.scalar.activation(ps[:, bank, 0:n], ps[:, bank, 0:n], ACT.Sqrt, bias=eps,
                                     scale=1.0 / D).then_inc(rt_done, 1)

            def norm_hi(nn, n):
                for c in range(KD):
                    act.wait_ge(xn_done, KD * nn + c + 1)
                    nc.scalar.activation(n_hi[:, c, 0:n], xn[:, c * T:c * T + n], ACT.Copy).then_inc(nh_done, 1)

            act.wait_ge(xT_ready, 2)
            nc.scalar.activation(X[:, 0:4, 0:P], ps[:, 0, :].rearrange("p (k t) -> p k t", k=4), ACT.Copy).then_inc(x_act, 1)
            act.wait_ge(xT_ready, 4)
            nc.scalar.activation(X[:, 0:4, P:2 * P], ps[:, 2, :].rearrange("p (k t) -> p k t", k=4), ACT.Copy).then_inc(x_act, 1)
            act.wait_ge(xT_ready, 6)
            nc.scalar.activation(X[:, :, 2 * P:T], ps[:, 4, 0:KD * (T - 2 * P)].rearrange("p (k t) -> p k t", k=KD),
                                 ACT.Copy).then_inc(x_act, 1)
            act.wait_ge(x_act, 3)
            act.wait_ge(x_dve, 3)
            for c in range(KD):
                nc.scalar.activation(xn[:, c * T:(c + 1) * T], X[:, c, :], ACT.Square).then_inc(sq_done, 1)
            act.wait_ge(consts, 8)
            root(0, 7, T)
            hi(0)
            hi(1)
            norm_hi(0, NS)
            for q in range(2, 2 + LEAD):
                hi(q)
            squares(1, OLD, NS)
            root(1, 4, NS)
            norm_hi(1, NS)

            sg = xn[:, 0:2 * 2 * NS].rearrange("p (b m t) -> p b m t", b=2, m=2)
            hf = xn[:, 2 * 2 * NS:4 * 2 * NS].rearrange("p (b m t) -> p b m t", b=2, m=2)

            act.wait_ge(nl_done, 2 * KD)
            with act.Fori(0, 2) as it:
                for n in range(STEPS):
                    q = 2 * G_GU + 4 * n + LEAD
                    hi(q, 2 * it)
                    hi(q + 1, 2 * it)
                    act.wait_ge(sub_done, 2 * G_GU + 4 * (STEPS * it + n) + 2)
                    act.wait_ge(dmul, 1 + STEPS * it + (n - 1 if n >= 2 else 0))
                    b = n % 2
                    nc.scalar.activation(sg[:, b], ps[:, 4 * b:4 * b + 2, 0:NS], ACT.Silu).then_inc(dsilu, 1)
                    hi(q + 2, 2 * it)
                    hi(q + 3, 2 * it)
                    act.wait_ge(dmul, 1 + STEPS * it + n + 1)
                    nc.scalar.activation(hid_hi[:, bass.ds(2 * STEPS * it + 2 * n, 2), :], hf[:, b], ACT.Copy).then_inc(dhid_hi, 1)

            q = 2 * G_DN + LEAD
            for _ in range(2 * STEPS):
                hi(q)
                q += 1
            squares(2, OLD, NS, range(4))
            for _ in range(2 * STEPS):
                hi(q)
                q += 1
            squares(2, OLD, NS, range(4, KD))
            root(2, 7, NS)
            norm_hi(2, NS)

            cs = xn[:, 0:2 * NS].rearrange("p (m t) -> p m t", m=2)
            zf = xn[:, 6 * NS:6 * NS + 2 * SEQ].rearrange("p (m t) -> p m t", m=2)
            act.wait_ge(nl_done, 3 * KD)
            for j in range(KD // 2):
                hi(q)
                hi(q + 1)
                act.wait_ge(sub_done, 2 * G_CI + 6 * j + 2)
                if j:
                    act.wait_ge(u_made, j)
                nc.scalar.activation(cs, ps[:, 0:2, 0:NS], ACT.Copy).then_inc(c_copied, 1)
                for i in range(2, 6):
                    hi(q + i)
                q += 6
                act.wait_ge(z_made, j + 1)
                nc.scalar.activation(hid_hi[:, 2 * j:2 * j + 2, 0:SEQ], zf, ACT.Copy).then_inc(z_hi_done, 1)
            while q < Q_MOE:
                hi(q)
                q += 1
            act.wait_ge(rout_in, 16)
            nc.scalar.activation(r_hi[:, :, :], r32[:, :, :], ACT.Copy).then_inc(rh_done, 1)
            squares(3, N_META, SEQ)
            root(3, 6, SEQ)
            norm_hi(3, SEQ)
            act.wait_ge(nl_done, 4 * KD)
            for i in range(2 * TT):
                act.wait_ge(rT_ready, i + 1)
                nc.scalar.activation(racc[:, i // 2, 512 * (i % 2):512 * (i % 2) + 512], ps[:, i, :],
                                     ACT.Copy).then_inc(racc_done, 1)
            act.wait_ge(dlog, 1)
            nc.scalar.activation(gw[:, 1, :], gw[:, 0, :], ACT.Exp).then_inc(elog, 1)
            for i in range(2 * TT):
                act.wait_ge(hnT_ready, i + 1)
                nc.scalar.activation(hn_hi[:, i // 2, 512 * (i % 2):512 * (i % 2) + 512],
                                     ps[:, (4, 5, 7, 0)[i], :], ACT.Copy).then_inc(hn_hi_done, 1)
            act.wait_ge(hnT_ready, 4 * TT)
            act.dma_start(gfin[:, :], final_norm.rearrange("(a d) -> a d", a=1).to_broadcast([P, D])).then_inc(gfin_in, 16)

            def gathered(t):
                act.wait_ge(gath_ready, t + 1)
                nc.scalar.activation(xg_hi[:, :, :], ps[:, 6:8, :], ACT.Copy).then_inc(xgh_done, 1)

            def y_high(t):
                act.wait_ge(sub_done, Q_MOE + PASS_S * t)
                act.wait_ge(gs_done, 1 + t)
                nc.scalar.activation(y_hi[:, :], ps[:, 4:6, :], ACT.Copy, scale=slot_gate).then_inc(yh_done, 1)

            act.wait_ge(arena_zero, 4)
            act.wait_ge(y_zero, 1)
            gathered(0)
            act.wait_ge(route_done, 1)
            n_pass = act.value_load(npass[0:1, 0:1], min_val=E, max_val=2 * E)
            with act.Fori(0, n_pass) as t:
                turns = t * (PASS_S // (2 * RING))
                for r in range(PASS_S):
                    if r == 3:
                        y_high(t)
                    for s in range(STEPS):
                        if r == up_step(s) + 7:
                            act.wait_ge(sub_done, Q_MOE + PASS_S * t + up_step(s) + 4)
                            act.wait_ge(mul_done, 1 + STEPS * t + s)
                            nc.scalar.activation(silu_m[:, :], ps[:, 0, :], ACT.Silu).then_inc(silu_done, 1)
                        if r == turn_after(s) + 3:
                            act.wait_ge(t_ready, STEPS * t + s + 1)
                            nc.scalar.activation(mT_hi[:, :, :], ps[:, 2, :], ACT.Copy).then_inc(mTh_done, 1)
                    if r == up_end(2) + 4:
                        act.wait_ge(pt_ready, t + 1)
                        nc.scalar.activation(pickT[:, :, :], ps[:, 3, 0:TT * P], ACT.Copy).then_inc(pT_done, 1)
                    if r == PASS_S - 1:
                        gathered(t + 1)
                    hi(Q_MOE + r, turns)
            y_high(n_pass)
            act.wait_ge(comb_added, TT * n_pass + TT)
            for tt in range(TT):
                nc.scalar.activation(junk[:, :], racc[:, tt, :], ACT.Square, accum_out=ssum[:, tt:tt + 1]).then_inc(ss_fin, 1)
                act.wait_ge(ss_fin, tt + 1)
            nc.scalar.activation(rstd, ssum, ACT.Sqrt, bias=eps, scale=1.0 / D).then_inc(rt_fin, 1)

        @block.vector
        def _(dve):
            dve.sem_inc(dmul, 1)
            dve.sem_inc(dhid_lo, 1)
            dve.sem_inc(mul_done, 1)
            dve.sem_inc(gs_done, 1)
            steps = [0]

            def link(ins):
                steps[0] += 1
                ins.then_inc(dve_step, 1)
                dve.wait_ge(dve_step, steps[0])

            def lo(q, turns=0):
                dve.wait_ge(hi_done, q + 1 + 2 * RING * turns)
                nc.vector.tensor_tensor(w_lo[:, q % RING, :],
                                        raw[:, raw_slot(q // 2), (q % 2) * SUB:(q % 2 + 1) * SUB],
                                        w_hi[:, q % RING, :].bitcast(F32), ALU.subtract).then_inc(lo_done, 1)

            def norm_lo(nn, c, n):
                dve.wait_ge(nh_done, KD * nn + c + 1)
                nc.vector.tensor_tensor(n_lo[:, c, 0:n], xn[:, c * T:c * T + n], n_hi[:, c, 0:n].bitcast(F32),
                                        ALU.subtract).then_inc(nl_done, 1)

            def norm(nn, bank, col, n, gain):
                dve.wait_ge(rt_done, nn + 1)
                link(nc.vector.reciprocal(ps[:, bank, 0:n], ps[:, bank, 0:n]))
                for c in range(KD):
                    nc.vector.scalar_tensor_tensor(out=xn[:, c * T:c * T + n], in0=X[:, c, col:col + n],
                                                   scalar=prm[:, gain + c:gain + c + 1], in1=ps[:, bank, 0:n],
                                                   op0=ALU.mult, op1=ALU.mult).then_inc(xn_done, 1)
                    if c:
                        norm_lo(nn, c - 1, n)
                norm_lo(nn, KD - 1, n)

            dve.wait_ge(xT_ready, 1)
            nc.vector.tensor_copy(prm[:, :], ps[:, 6, 0:64]).then_inc(x_dve, 1)
            dve.wait_ge(xT_ready, 3)
            nc.vector.tensor_copy(X[:, 4:8, 0:P], ps[:, 1, :].rearrange("p (k t) -> p k t", k=4)).then_inc(x_dve, 1)
            dve.wait_ge(xT_ready, 5)
            nc.vector.tensor_copy(X[:, 4:8, P:2 * P], ps[:, 3, :].rearrange("p (k t) -> p k t", k=4)).then_inc(x_dve, 1)
            lo(0)
            lo(1)
            dve.wait_ge(x_dve, 3)
            dve.wait_ge(rt_done, 1)
            link(nc.vector.reciprocal(ps[:, 7, 0:T], ps[:, 7, 0:T]))
            for c in range(KD):
                w = WINDOWS[c * P // GW]
                if c:
                    dve.wait_ge(xn_done, c)
                link(nc.vector.scalar_tensor_tensor(out=hp[:, 1:1 + T], in0=X[:, c, :],
                                                    scalar=prm[:, PN + c:PN + c + 1], in1=ps[:, 7, 0:T],
                                                    op0=ALU.mult, op1=ALU.mult))
                src, dst, reach, first = hp, sa, 1, 0
                while reach < w:
                    first += reach
                    link(nc.vector.tensor_tensor(dst[:, first:1 + T], src[:, first:1 + T],
                                                 src[:, first - reach:1 + T - reach], ALU.add))
                    src, dst = dst, (sb if dst is sa else sa)
                    reach *= 2
                o = xn[:, c * T:c * T + NS]
                ins = nc.vector.scalar_tensor_tensor(out=o, in0=src[:, 1 + OLD:1 + T], scalar=1.0 / w,
                                                     in1=hp[:, 1 + OLD:1 + T], op0=ALU.mult, op1=ALU.subtract)
                for k in range(max(0, w - 1 - OLD)):
                    link(ins)
                    ins = nc.vector.scalar_tensor_tensor(out=o[:, k:k + 1], in0=src[:, 1 + OLD + k:2 + OLD + k],
                                                         scalar=1.0 / (OLD + k + 1),
                                                         in1=hp[:, 1 + OLD + k:2 + OLD + k],
                                                         op0=ALU.mult, op1=ALU.subtract)
                ins.then_inc(xn_done, 1)
                if c:
                    norm_lo(0, c - 1, NS)
            norm_lo(0, KD - 1, NS)
            for q in range(2, 2 + LEAD):
                lo(q)
            for c in range(KD):
                dve.wait_ge(sub_done, c // 4 + 1)
                nc.vector.scalar_tensor_tensor(out=X[:, c, OLD:T], in0=ps[:, c, 0:NS],
                                               scalar=prm[:, PS + c:PS + c + 1], in1=X[:, c, OLD:T],
                                               op0=ALU.mult, op1=ALU.add).then_inc(x_new, 1)
            norm(1, 4, OLD, NS, DN)

            sg = xn[:, 0:2 * 2 * NS].rearrange("p (b m t) -> p b m t", b=2, m=2)
            hf = xn[:, 2 * 2 * NS:4 * 2 * NS].rearrange("p (b m t) -> p b m t", b=2, m=2)
            with dve.Fori(0, 2) as it:
                for n in range(STEPS):
                    q = 2 * G_GU + 4 * n + LEAD
                    lo(q, 2 * it)
                    lo(q + 1, 2 * it)
                    lo(q + 2, 2 * it)
                    b = n % 2
                    dve.wait_ge(dsilu, STEPS * it + n + 1)
                    dve.wait_ge(sub_done, 2 * G_GU + 4 * (STEPS * it + n) + 4)
                    dve.wait_ge(dhid_lo, 1 + STEPS * it + (n - 1 if n >= 2 else 0))
                    nc.vector.tensor_tensor(hf[:, b], sg[:, b], ps[:, 4 * b + 2:4 * b + 4, 0:NS],
                                            ALU.mult).then_inc(dmul, 1)
                    lo(q + 3, 2 * it)
                    dve.wait_ge(dhid_hi, STEPS * it + n + 1)
                    at_ = bass.ds(2 * STEPS * it + 2 * n, 2)
                    nc.vector.tensor_tensor(hid_lo[:, at_, :], hf[:, b], hid_hi[:, at_, :].bitcast(F32),
                                            ALU.subtract).then_inc(dhid_lo, 1)
            q = 2 * G_DN + LEAD
            for half in range(2):
                for _ in range(2 * STEPS):
                    lo(q)
                    q += 1
                for c in range(4 * half, 4 * half + 4):
                    if c % 4 < 3:
                        dve.wait_ge(dn_ready, 3 * half + c % 4 + 1)
                    else:
                        dve.wait_ge(sub_done, 2 * G_DN + 2 * STEPS * (half + 1))
                    nc.vector.tensor_tensor(X[:, c, OLD:T], ps[:, (c + 4) % 8, 0:NS], X[:, c, OLD:T], ALU.add).then_inc(x_new, 1)
            norm(2, 7, OLD, NS, CN)
            cs = xn[:, 0:2 * NS].rearrange("p (m t) -> p m t", m=2)
            u = xn[:, 2 * NS:4 * NS].rearrange("p (m t) -> p m t", m=2)
            y = xn[:, 4 * NS:4 * NS + 2 * SEQ].rearrange("p (m t) -> p m t", m=2)
            zf = xn[:, 6 * NS:6 * NS + 2 * SEQ].rearrange("p (m t) -> p m t", m=2)
            for j in range(KD // 2):
                lo(q)
                lo(q + 1)
                lo(q + 2)
                lo(q + 3)
                dve.wait_ge(c_copied, j + 1)
                dve.wait_ge(sub_done, 2 * G_CI + 6 * j + 4)
                ins = nc.vector.tensor_tensor(u, cs, ps[:, 2:4, 0:NS], ALU.mult)
                ins.then_inc(u_made, 1)
                dve.wait_ge(u_made, j + 1)
                if j:
                    dve.wait_ge(z_made, j)
                for m in range(2):
                    for k in range(TAPS):
                        tap = prm[:, CK + KD * k + 2 * j + m:CK + KD * k + 2 * j + m + 1]
                        if k == 0:
                            link(nc.vector.tensor_scalar(y[:, m], u[:, m, 0:SEQ], tap, None, ALU.mult))
                        else:
                            link(nc.vector.scalar_tensor_tensor(out=y[:, m], in0=u[:, m, k:k + SEQ], scalar=tap,
                                                                in1=y[:, m], op0=ALU.mult, op1=ALU.add))
                lo(q + 4)
                lo(q + 5)
                q += 6
                dve.wait_ge(sub_done, 2 * G_CI + 6 * j + 6)
                if j:
                    dve.wait_ge(z_lo_done, j)
                nc.vector.tensor_tensor(zf, y, ps[:, 4:6, TAPS - 1:NS], ALU.mult).then_inc(z_made, 1)
                dve.wait_ge(z_hi_done, j + 1)
                nc.vector.tensor_tensor(hid_lo[:, 2 * j:2 * j + 2, 0:SEQ], zf,
                                        hid_hi[:, 2 * j:2 * j + 2, 0:SEQ].bitcast(F32), ALU.subtract).then_inc(z_lo_done, 1)
            while q < Q_MOE:
                lo(q)
                q += 1
            dve.wait_ge(rh_done, 1)
            nc.vector.tensor_tensor(r_lo[:, :, :], r32[:, :, :], r_hi[:, :, :].bitcast(F32), ALU.subtract).then_inc(rl_done, 1)
            for c in range(KD):
                if c % 2 == 0:
                    dve.wait_ge(co_ready, c // 2 + 1)
                else:
                    dve.wait_ge(sub_done, 2 * G_CO + c + 1)
                nc.vector.tensor_tensor(X[:, c, N_META:T], ps[:, (c + 6) % 8, 0:SEQ], X[:, c, N_META:T],
                                        ALU.add).then_inc(x_new, 1)
            norm(3, 6, N_META, SEQ, MN)

            dve.wait_ge(consts, 8)
            dve.wait_ge(lg_ready, 1)
            link(nc.vector.tensor_copy(lg[:, :, :], ps[:, 6, 0:TT * E].rearrange("p (a e) -> p a e", a=TT)))
            for tt in range(TT):
                link(nc.vector.max(mx[:, tt, :], lg[:, tt, :]))
                link(nc.vector.max_index(ix[:, tt, :], mx[:, tt, :], lg[:, tt, :]))
            nc.vector.tensor_tensor(gw[:, 0, :], mx[:, :, 1], mx[:, :, 0], ALU.subtract).then_inc(dlog, 1)
            link(nc.vector.tensor_copy(ixf[:, :, :], ix[:, :, :]))
            for tt in range(TT):
                nc.vector.tensor_scalar(oh1[:, tt, :], iota[:, 0:E], ixf[:, tt, 0:1], None, ALU.is_equal)
                link(nc.vector.tensor_scalar(oh2[:, tt, :], iota[:, 0:E], ixf[:, tt, 1:2], None, ALU.is_equal))
            nc.vector.tensor_tensor(mask[:, :, :], oh1[:, :, :], oh2[:, :, :], ALU.add).then_inc(mask_done, 1)
            dve.wait_ge(elog, 1)
            link(nc.vector.tensor_scalar(gw[:, 2, :], gw[:, 1, :], 1.0, None, ALU.add))
            link(nc.vector.reciprocal(gw[:, 2, :], gw[:, 2, :]))
            link(nc.vector.tensor_tensor(gw[:, 3, :], gw[:, 1, :], gw[:, 2, :], ALU.mult))
            for tt in range(TT):
                link(nc.vector.tensor_scalar(gates[:, tt, :], oh1[:, tt, :], gw[:, 2, tt:tt + 1], None, ALU.mult))
                link(nc.vector.scalar_tensor_tensor(out=gates[:, tt, :], in0=oh2[:, tt, :], scalar=gw[:, 3, tt:tt + 1],
                                                    in1=gates[:, tt, :], op0=ALU.mult, op1=ALU.add))
            dve.wait_ge(mask_done, 1)
            dve.wait_ge(pos_ready, 1)
            link(nc.vector.scalar_tensor_tensor(out=rank[:, :, :], in0=ps[:, 6, 32:32 + TT * E].rearrange("p (a e) -> p a e", a=TT),
                                                scalar=1.0, in1=mask[:, :, :], op0=ALU.add, op1=ALU.mult))
            nc.vector.tensor_scalar(slot_of[:, :, E:2 * E], rank[:, :, :], -1.0 - P, None, ALU.add)
            link(nc.vector.tensor_scalar(slot_of[:, :, 0:E], rank[:, :, :], -1.0, None, ALU.add))

            def make_pick(t):
                for tt in range(TT):
                    ins = nc.vector.tensor_scalar(pick[:, tt, :], iota[:, :], slot_of[:, tt, bass.ds(t, 1)], None,
                                                  ALU.is_equal)
                ins.then_inc(pick_done, 1)

            dve.wait_ge(arena_zero, 4)
            make_pick(0)
            link(nc.vector.tensor_reduce(cmax, ps[:, 6, 64:64 + E], AX_X, ALU.max))
            link(nc.vector.tensor_scalar(cmax, cmax, float(P), float(E), ALU.is_gt, ALU.mult))
            nc.vector.tensor_scalar(npass[:, :], cmax, float(E), None, ALU.add).then_inc(route_done, 1)
            for i in range(2 * TT):
                dve.wait_ge(hnT_ready, 2 * TT + i + 1)
                nc.vector.tensor_copy(hn_lo[:, i // 2, 512 * (i % 2):512 * (i % 2) + 512],
                                      ps[:, (1, 2, 3, 4)[i], :]).then_inc(hn_lo_done, 1)

            def gathered(t):
                dve.wait_ge(gath_ready, t + 1)
                nc.vector.tensor_copy(xg_lo[:, 0:4, :], ps[:, 3, :].rearrange("p (k t) -> p k t", k=4))
                nc.vector.tensor_copy(xg_lo[:, 4:8, :], ps[:, 0, :].rearrange("p (k t) -> p k t", k=4)).then_inc(xgl_done, 1)

            def y_low(t):
                dve.wait_ge(yh_done, t + 1)
                nc.vector.scalar_tensor_tensor(out=y_lo[:, :], in0=ps[:, 4:6, :].rearrange("p a n -> p (a n)"), scalar=slot_gate,
                                               in1=y_hi[:, :].bitcast(F32), op0=ALU.mult,
                                               op1=ALU.subtract).then_inc(yl_done, 1)

            def combined(t):
                for tt in range(TT):
                    b = (6, 2)[tt]
                    dve.wait_ge(comb_ready, TT * t + tt + 1)
                    nc.vector.tensor_tensor(racc[:, tt, :], ps[:, b:b + 2, :].rearrange("p a n -> p (a n)"),
                                            racc[:, tt, :], ALU.add).then_inc(comb_added, 1)

            gathered(0)
            dve.wait_ge(route_done, 1)
            n_pass = dve.value_load(npass[0:1, 0:1], min_val=E, max_val=2 * E)
            with dve.Fori(0, n_pass) as t:
                turns = t * (PASS_S // (2 * RING))
                for r in range(PASS_S):
                    if r == 3:
                        y_low(t)
                    if r == 7 + 3:
                        combined(t)
                    for s in range(STEPS):
                        if r == up_end(s) + 3:
                            dve.wait_ge(silu_done, 1 + STEPS * t + s + 1)
                            dve.wait_ge(sub_done, Q_MOE + PASS_S * t + up_end(s) + 1)
                            nc.vector.tensor_tensor(hid_m[:, :], silu_m[:, :], ps[:, 1, :], ALU.mult).then_inc(mul_done, 1)
                        if r == turn_after(s) + 3:
                            dve.wait_ge(mTh_done, STEPS * t + s + 1)
                            nc.vector.tensor_tensor(mT_lo[:, :, :], ps[:, 2, :].rearrange("p (k t) -> p k t", k=4),
                                                    mT_hi[:, :, :].bitcast(F32), ALU.subtract).then_inc(mTl_done, 1)
                    if r == up_end(2) + 3:
                        dve.wait_ge(pT_done, 1 + t + 1)
                        nc.vector.tensor_copy(slot_gate, ps[:, 3, TT * P:TT * P + 1]).then_inc(gs_done, 1)
                        make_pick(t + 1)
                    if r == PASS_S - 1:
                        gathered(t + 1)
                    lo(Q_MOE + r, turns)
            y_low(n_pass)
            combined(n_pass)
            dve.wait_ge(rt_fin, 1)
            dve.wait_ge(gfin_in, 16)
            link(nc.vector.reciprocal(rstd, rstd))
            for tt in range(TT):
                nc.vector.scalar_tensor_tensor(out=racc[:, tt, :], in0=racc[:, tt, :], scalar=rstd[:, tt:tt + 1],
                                               in1=gfin[:, :], op0=ALU.mult, op1=ALU.mult).then_inc(o_done, 1)

        @block.tensor
        def _(pe):
            mm = nc.tensor.matmul

            def use(q, turns=0):
                pe.wait_ge(lo_done, q + 1 + 2 * RING * turns)

            def features(bank, n, sub_col, q, mov_hi, mov_lo, first, last):
                wh = w_hi[:, q % RING, sub_col:sub_col + P]
                wl = w_lo[:, q % RING, sub_col:sub_col + P]
                mm(ps[:, bank, 0:n], wh, mov_hi, start=first, stop=False)
                mm(ps[:, bank, 0:n], wh, mov_lo, start=False, stop=False)
                return mm(ps[:, bank, 0:n], wl, mov_hi, start=False, stop=last)

            def mean_square(nn, bank, n):
                for c in range(KD):
                    pe.wait_ge(sq_done, KD * nn + c + 1)
                    last = mm(ps[:, bank, 0:n], ones[:, :], xn[:, c * T:c * T + n], start=(c == 0), stop=(c == KD - 1))
                last.then_inc(ss_ready, 1)

            pe.wait_ge(consts, 8)
            pe.wait_ge(prm_in, 16 * 6)
            nc.tensor.transpose(ps[:, 6, 0:64], param_rows[:, :], ident[0:64, 0:64]).then_inc(xT_ready, 1)
            pe.wait_ge(tok_in, 16 * 4)
            for a in range(2):
                for h in range(2):
                    for k in range(4):
                        c = 4 * h + k
                        last = nc.tensor.transpose(ps[:, 2 * a + h, k * P:(k + 1) * P], tok[:, a, c * P:(c + 1) * P], ident[:, :])
                    last.then_inc(xT_ready, 1)
            R = T - 2 * P
            for c in range(KD):
                last = nc.tensor.transpose(ps[:, 4, c * R:(c + 1) * R], tok[0:R, 2, c * P:(c + 1) * P], ident[0:R, 0:R])
            last.then_inc(xT_ready, 1)
            mean_square(0, 7, T)

            for g in range(GROUPS):
                q = g // 2
                use(q)
                for m in range(2):
                    for k in range(2):
                        c = 2 * g + k
                        pe.wait_ge(nl_done, c + 1)
                        last = features(2 * g + m, NS, (g % 2) * 2 * GW + k * GW + m * P, q,
                                        n_hi[:, c, :], n_lo[:, c, :], k == 0, k == 1)
                if g % 2:
                    last.then_inc(sub_done, 1)

            pe.wait_ge(x_new, 5)
            mean_square(1, 4, NS)

            pe.wait_ge(nh_done, 2 * KD)
            with pe.Fori(0, 2) as it:
                for n in range(STEPS):
                    q = 2 * G_GU + 4 * n
                    b = 4 * (n % 2)
                    pe.wait_ge(dmul, 1 + STEPS * it + (n - 1 if n >= 2 else 0))
                    for part in range(2):
                        for s in range(2):
                            use(q, 2 * it)
                            for m in range(2):
                                for k in range(4):
                                    c = 4 * s + k
                                    if n == 0 and part == 0:
                                        pe.wait_ge(nl_done, KD + c + 1)
                                    last = features(b + 2 * part + m, NS, k * 256 + m * P, q, n_hi[:, c, :], n_lo[:, c, :],
                                                    c == 0, c == KD - 1)
                            last.then_inc(sub_done, 1)
                            q += 1
            q = 2 * G_DN
            for half in range(2):
                pe.wait_ge(dmul, 1 + 2 * STEPS - 1 + half)
                for i in range(2 * STEPS):
                    use(q)
                    if half == 0:
                        pe.wait_ge(dhid_lo, 1 + i + 1)
                    for c in range(4):
                        for k in range(2):
                            f = 2 * i + k
                            last = features((4 * half + c + 4) % 8, NS, k * 512 + c * P, q, hid_hi[:, f, :], hid_lo[:, f, :],
                                            f == 0, f == KF - 1)
                        if i == 2 * STEPS - 1 and c < 3:
                            last.then_inc(dn_ready, 1)
                    last.then_inc(sub_done, 1)
                    q += 1
            pe.wait_ge(x_new, KD + 4)
            mean_square(2, 7, NS)
            for j in range(KD // 2):
                for part in range(3):
                    for s in range(2):
                        use(q)
                        if j and s == 0:
                            pe.wait_ge((c_copied, u_made, z_made)[part], j)
                        for m in range(2):
                            for k in range(4):
                                c = 4 * s + k
                                if j == 0 and part == 0 and m == 0:
                                    pe.wait_ge(nl_done, 2 * KD + c + 1)
                                last = features(2 * part + m, NS, k * 256 + m * P, q, n_hi[:, c, :], n_lo[:, c, :],
                                                c == 0, c == KD - 1)
                        last.then_inc(sub_done, 1)
                        q += 1
            for i in range(KD // 2):
                if i == 1:
                    pe.wait_ge(z_made, KD // 2)
                for s in range(2):
                    use(q)
                    for m in range(2):
                        for k in range(4):
                            c = 4 * s + k
                            if i == 0 and m == 0:
                                pe.wait_ge(z_lo_done, c // 2 + 1)
                            last = features((2 * i + m + 6) % 8, SEQ, k * 256 + m * P, q, hid_hi[:, c, 0:SEQ],
                                            hid_lo[:, c, 0:SEQ], c == 0, c == KD - 1)
                        if s == 1 and m == 0:
                            last.then_inc(co_ready, 1)
                    last.then_inc(sub_done, 1)
                    q += 1
            mean_square(3, 6, SEQ)
            for i in range(2 * TT):
                tt, h = divmod(i, 2)
                for k in range(4):
                    c = 4 * h + k
                    last = nc.tensor.transpose(ps[:, i, k * P:(k + 1) * P], X[:, c, N_META + tt * P:N_META + (tt + 1) * P],
                                               ident[:, :])
                last.then_inc(rT_ready, 1)
            pe.wait_ge(rl_done, 1)
            pe.wait_ge(xn_done, 4 * KD)
            for tt in range(TT):
                for c in range(KD):
                    pe.wait_ge(nl_done, 3 * KD + c + 1)
                    o = ps[:, 6, tt * E:(tt + 1) * E]
                    tok_hi = n_hi[:, c, tt * P:(tt + 1) * P]
                    tok_lo = n_lo[:, c, tt * P:(tt + 1) * P]
                    mm(o, tok_hi, r_hi[:, c, :], start=(c == 0), stop=False)
                    mm(o, tok_hi, r_lo[:, c, :], start=False, stop=False)
                    last = mm(o, tok_lo, r_hi[:, c, :], start=False, stop=(c == KD - 1))
            last.then_inc(lg_ready, 1)

            def turn_normed(n, i, bank):
                tt, h = divmod(i, 2)
                for k in range(4):
                    c = 4 * h + k
                    last = nc.tensor.transpose(ps[:, bank, k * P:(k + 1) * P],
                                               n[:, c, tt * P:(tt + 1) * P].bitcast(F32), ident[:, :])
                last.then_inc(hnT_ready, 1)

            turn_normed(n_hi, 0, 4)
            turn_normed(n_hi, 1, 5)
            turn_normed(n_hi, 2, 7)
            pe.wait_ge(mask_done, 1)
            for tt in range(TT):
                o = ps[:, 6, 32 + tt * E:32 + (tt + 1) * E]
                for s in range(tt):
                    mm(o, ones[:, :], mask[:, s, :], start=(s == 0), stop=False)
                mm(o, before[:, :], mask[:, tt, :], start=(tt == 0), stop=True)
            for tt in range(TT):
                last = mm(ps[:, 6, 64:64 + E], ones[:, :], mask[:, tt, :], start=(tt == 0), stop=(tt == TT - 1))
            last.then_inc(pos_ready, 1)
            pe.wait_ge(racc_done, 4)
            turn_normed(n_hi, 3, 0)
            turn_normed(n_lo, 0, 1)
            turn_normed(n_lo, 1, 2)
            turn_normed(n_lo, 2, 3)
            pe.wait_ge(hn_hi_done, 1)
            turn_normed(n_lo, 3, 4)
            pe.wait_ge(arena_zero, 4)
            pe.wait_ge(hn_hi_done, 4)
            pe.wait_ge(hn_lo_done, 4)
            for h in range(2):
                last = mm(ps[:, 4 + h, :], y_hi[:, 0:P], y_lo[:, 0:512], start=True, stop=True)
            last.then_inc(y_zero, 1)

            def gather(t):
                for src, banks in ((hn_hi, (6, 7)), (hn_lo, (3, 0))):
                    for c in range(KD):
                        for tt in range(TT):
                            last = mm(ps[:, banks[c // 4], (c % 4) * P:(c % 4 + 1) * P], src[:, tt, c * P:(c + 1) * P],
                                      pick[:, tt, :], start=(tt == 0), stop=(tt == TT - 1))
                last.then_inc(gath_ready, 1)

            def combine(t):
                pe.wait_ge(yl_done, t + 1)
                pe.wait_ge(pT_done, 1 + t)
                for tt in range(TT):
                    for h in range(2):
                        o = ps[:, (6, 2)[tt] + h, :]
                        mm(o, pickT[:, tt, :], y_hi[:, 512 * h:512 * h + 512], start=True, stop=False)
                        last = mm(o, pickT[:, tt, :], y_lo[:, 512 * h:512 * h + 512], start=False, stop=True)
                    last.then_inc(comb_ready, 1)

            def stream(bank, q, turns, piece, k, tok_hi, tok_lo, first, last_one):
                o = ps[:, bank, :]
                wh = w_hi[:, q % RING, piece * 512:piece * 512 + 512]
                wl = w_lo[:, q % RING, piece * 512:piece * 512 + 512]
                mm(o, tok_hi, wh, start=first, stop=False)
                mm(o, tok_hi, wl, start=False, stop=False)
                return mm(o, tok_lo, wh, start=False, stop=last_one)

            pe.wait_ge(pick_done, 1)
            pe.wait_ge(route_done, 1)
            gather(0)
            n_pass = pe.value_load(npass[0:1, 0:1], min_val=E, max_val=2 * E)
            with pe.Fori(0, n_pass) as t:
                turns = t * (PASS_S // (2 * RING))
                r = 0

                def up_like(bank):
                    nonlocal r
                    for i in range(4):
                        q = Q_MOE + r
                        use(q, turns)
                        for k in range(2):
                            c = 2 * i + k
                            last = stream(bank, q, turns, k, k, xg_hi[:, c, :], xg_lo[:, c, :], c == 0, c == KD - 1)
                        last.then_inc(sub_done, 1)
                        r += 1

                def turn_hidden(s):
                    pe.wait_ge(mul_done, 1 + STEPS * t + s + 1)
                    if s == 0:
                        pe.wait_ge(comb_added, TT * t + TT)
                    for k in range(4):
                        last = nc.tensor.transpose(ps[:, 2, k * P:(k + 1) * P], hid_m[:, k * P:(k + 1) * P], ident[:, :])
                    last.then_inc(t_ready, 1)

                def down(s):
                    nonlocal r
                    pe.wait_ge(mTl_done, STEPS * t + s + 1)
                    for k in range(4):
                        q = Q_MOE + r
                        use(q, turns)
                        for h in range(2):
                            last = stream(4 + h, q, turns, h, k, mT_hi[:, k, :], mT_lo[:, k, :], s == 0 and k == 0,
                                          s == STEPS - 1 and k == 3)
                        last.then_inc(sub_done, 1)
                        r += 1

                for s in range(STEPS):
                    if s == 0:
                        pe.wait_ge(xgh_done, t + 1)
                        pe.wait_ge(xgl_done, t + 1)
                    pe.wait_ge(silu_done, 1 + STEPS * t + s)
                    up_like(0)
                    if s >= 1:
                        turn_hidden(s - 1)
                    pe.wait_ge(mul_done, 1 + STEPS * t + s)
                    up_like(1)
                    if s == 0:
                        combine(t)
                    if s == 2:
                        pe.wait_ge(comb_added, TT * t + TT)
                        for tt in range(TT):
                            nc.tensor.transpose(ps[:, 3, tt * P:(tt + 1) * P], pick[:, tt, :].bitcast(F32), ident[:, :])
                        for tt in range(TT):
                            last = mm(ps[:, 3, TT * P:TT * P + 1], pick[:, tt, :].bitcast(F32),
                                      gates[:, tt, bass.ds(t % E, 1)], start=(tt == 0), stop=(tt == TT - 1))
                        last.then_inc(pt_ready, 1)
                    if s >= 1:
                        down(s - 1)
                pe.wait_ge(pick_done, t + 2)
                pe.wait_ge(pT_done, 1 + t + 1)
                pe.wait_ge(gs_done, 1 + t + 1)
                pe.wait_ge(silu_done, 1 + STEPS * t + STEPS)
                gather(t + 1)
                turn_hidden(STEPS - 1)
                down(STEPS - 1)
            combine(n_pass)


_INS = ["x", "meta_tokens", "pool_norm", "pool_w", "pool_scale", "dense_norm", "dense_w_gate", "dense_w_up",
        "dense_w_down", "conv_norm", "conv_w_in", "conv_kernel", "conv_w_out", "moe_norm", "moe_router",
        "moe_w_gate", "moe_w_up", "moe_w_down", "final_norm"]


def kernel(**inputs):
    import numpy as np
    import concourse.bacc as bacc
    from concourse import mybir as mb
    from concourse.bass_utils import run_bass_kernel_spmd

    nc = bacc.Bacc("TRN2", target_bir_lowering=False, num_devices=1)
    arrays, args = {}, []
    for name in _INS:
        a = np.ascontiguousarray(inputs[name])
        arrays[name] = a
        args.append(nc.dram_tensor(name, a.shape, mb.dt.from_np(a.dtype), kind="ExternalInput").ap())
    o = nc.dram_tensor("out", arrays["x"].shape, mb.dt.from_np(arrays["x"].dtype), kind="ExternalOutput").ap()
    build_encoder(nc, *args, o)
    r = run_bass_kernel_spmd(nc, [arrays], core_ids=[0])
    return r.results[0]["out"]
```

```python
from contextlib import ExitStack

import concourse.bass as bass
from concourse import mybir

ACT = mybir.ActivationFunctionType
ALU = mybir.AluOpType
AX_X = mybir.AxisListType.X
F32 = mybir.dt.float32
F32R = mybir.dt.float32r
I32 = mybir.dt.int32
U32 = mybir.dt.uint32

P = 128


def build_encoder(nc, x, meta_tokens, pool_norm, pool_w, pool_scale, dense_norm, dense_w_gate,
                  dense_w_up, dense_w_down, conv_norm, conv_w_in, conv_kernel, conv_w_out,
                  moe_norm, moe_router, moe_w_gate, moe_w_up, moe_w_down, final_norm, out):
    SEQ, D = x.shape[1], x.shape[2]
    N_META = meta_tokens.shape[0]
    T = SEQ + N_META
    F = dense_w_gate.shape[2]
    E = moe_router.shape[2]
    TAPS = conv_kernel.shape[1]
    GROUPS, GW = pool_w.shape[1], pool_w.shape[2]
    WINDOWS = (2, 4, 8, 16)
    EPS = 1e-6
    KD = D // P
    KF = F // P
    NS = SEQ + TAPS - 1
    OLD = T - NS
    TT = SEQ // P
    STEPS = F // 512
    assert (KD, TT, GW, GROUPS, E, KF, STEPS, TAPS) == (8, 2, 256, 4, 8, 28, 7, 3)

    RING = 7
    GRAN, SUB = 2048, 1024
    G_GU = 1
    G_DN = G_GU + 2 * KF // 2
    G_CI = G_DN + KF // 2
    G_CO = G_CI + 3 * D // 256
    G_MOE = G_CO + D // 256
    PASS_G = 6 * STEPS
    PASS_S = 2 * PASS_G
    Q_MOE = 2 * G_MOE
    LEAD = 4
    N_BANDS = 3 * len(WINDOWS) + 6
    BEHIND = 5
    assert PASS_G % RING == 0 and (4 * KF // 4) % RING == 0

    with ExitStack() as ctx:
        def sem(name):
            return ctx.enter_context(nc.semaphore(name))

        base = (nc.sbuf_base + 63) // 64 * 64
        at = [base]

        def region(nbytes):
            a = at[0]
            at[0] += (nbytes + 31) // 32 * 32
            return a

        def place(name, addr, shape, dt):
            return nc.alloc_sbuf_tensor_at(name, shape, dt, offset=addr)

        A_RAW, A_HI, A_LO = region(RING * GRAN * 4), region(RING * SUB * 4), region(RING * SUB * 4)
        A_AH, A_AL = region(KF * NS * 4), region(KF * NS * 4)
        A_NH, A_NL = region(KD * NS * 4), region(KD * NS * 4)
        A_XN, A_X = region(KD * T * 4), region(KD * T * 4)

        raw = place("raw", A_RAW, [P, RING, GRAN], F32)
        w_hi = place("w_hi", A_HI, [P, RING, SUB], F32R)
        w_lo = place("w_lo", A_LO, [P, RING, SUB], F32R)
        X = place("X", A_X, [P, KD, T], F32)
        xn = place("xn", A_XN, [P, KD * T], F32)
        n_hi = place("n_hi", A_NH, [P, KD, NS], F32R)
        n_lo = place("n_lo", A_NL, [P, KD, NS], F32R)
        hid_hi = place("hid_hi", A_AH, [P, KF, NS], F32R)
        hid_lo = place("hid_lo", A_AL, [P, KF, NS], F32R)
        param_rows = place("param_rows", A_AL, [64, P], F32)
        tok = place("tok", A_RAW + 5 * GRAN * 4, [P, 3, D], F32)
        tok_n = place("tok_n", A_AL + 512, [P, 3, D], F32)
        band = place("band", A_AH, [P, len(WINDOWS) + 1, T], F32)
        hn_hi = place("hn_hi", A_AH, [P, TT, D], F32R)
        hn_lo = place("hn_lo", A_AL, [P, TT, D], F32R)
        xg_hi = place("xg_hi", A_AH + 8192, [P, KD, P], F32R)
        xg_lo = place("xg_lo", A_AL + 8192, [P, KD, P], F32R)
        mT_hi = place("mT_hi", A_AH + 12288, [P, 4, P], F32R)
        mT_lo = place("mT_lo", A_AL + 12288, [P, 4, P], F32R)
        y_hi = place("y_hi", A_AH + 14336, [P, D], F32R)
        y_lo = place("y_lo", A_AL + 14336, [P, D], F32R)
        pick = place("pick", A_AH + 18432, [P, TT, P], F32R)
        pickT = place("pickT", A_AH + 19456, [P, TT, P], F32R)
        xg32 = place("xg32", A_NH, [P, KD, SEQ], F32)
        racc = place("racc", A_XN, [P, TT, D], F32)
        gfin = place("gfin", A_NH, [P, D], F32)
        silu_m = place("silu_m", A_NL, [P, 512], F32)
        hid_m = place("hid_m", A_NL + 2048, [P, 512], F32)
        junk = place("junk", A_X, [P, D], F32)

        ident = place("ident", region(512), [P, P], F32)
        ones = place("ones", region(512), [P, P], F32)
        before = place("before", region(512), [P, P], F32)
        iota = place("iota", region(512), [P, P], F32)
        prm = place("prm", region(256), [P, 64], F32)
        r32 = place("r32", region(256), [P, KD, E], F32)
        rs = place("rs", region(4 * NS), [P, 1, NS], F32)
        rs2 = place("rs2", region(4 * NS), [P, 1, NS], F32)
        lg = place("lg", region(64), [P, TT, E], F32)
        mx = place("mx", region(64), [P, TT, E], F32)
        ix = place("ix", region(64), [P, TT, E], U32)
        ixf = place("ixf", region(64), [P, TT, E], F32)
        oh1 = place("oh1", region(64), [P, TT, E], F32)
        oh2 = place("oh2", region(64), [P, TT, E], F32)
        mask = place("mask", region(64), [P, TT, E], F32)
        gates = place("gates", region(64), [P, TT, E], F32)
        slot_of = place("slot_of", region(160), [P, TT, 20], F32)
        rank = place("rank", region(64), [P, TT, E], F32)
        gw = place("gw", region(64), [P, 4, TT], F32)
        small = place("small", region(64), [P, 16], F32)
        npass = place("npass", region(32), [P, 1], I32)
        assert at[0] <= nc.sbuf_usable_end, at[0] - nc.sbuf_usable_end
        eps, cmax, ssum, rstd, slot_gate, tss = (small[:, 0:1], small[:, 1:2], small[:, 2:4],
                                                 small[:, 4:6], small[:, 6:7], small[:, 8:11])
        ps = ctx.enter_context(nc.psum_tensor("ps", [P, 8, 512], F32))

        RT_BANK, HT_BANK = (7, 0, 1, 2), (3, 4, 5, 7)
        PN, PS, DN, CN, MN, CK = 0, KD, 2 * KD, 3 * KD, 4 * KD, 5 * KD

        tok_in = [sem(f"tok_in{i}") for i in range(3)]
        prm_in, rout_in, gfin_in, out_done = (sem("prm_in"), sem("rout_in"),
                                                      sem("gfin_in"), sem("out_done"))
        raw_full = [sem(f"raw_full{i}") for i in range(RING)]
        hi_done, lo_done, sub_done = sem("hi_done"), sem("lo_done"), sem("sub_done")
        consts, xT_ready, x_act, x_dve = sem("consts"), sem("xT_ready"), sem("x_act"), sem("x_dve")
        dve_step = sem("dve_step")
        sq_done, ss_ready, rt_done, rs_done = sem("sq_done"), sem("ss_ready"), sem("rt_done"), sem("rs_done")
        tss_done, trt_done, trs_done, tn_act, tn_dve, bands, d_ready = (
            sem("tss_done"), sem("trt_done"), sem("trs_done"), sem("tn_act"), sem("tn_dve"), sem("bands"), sem("d_ready"))
        nh_done, nl_done, x_new = sem("nh_done"), sem("nl_done"), sem("x_new")
        dn_ready, co_ready = sem("dn_ready"), sem("co_ready")
        dgate, dup, dsilu, dmul, dhid_hi, dhid_lo = (sem("dgate"), sem("dup"), sem("dsilu"), sem("dmul"), sem("dhid_hi"),
                                                sem("dhid_lo"))
        c_taken, u_made, z_made, z_hi_done, z_lo_done = (
            sem("c_taken"), sem("u_made"), sem("z_made"), sem("z_hi_done"), sem("z_lo_done"))
        arena_zero, rT_ready, racc_done, hnT_ready, hn_hi_done, hn_lo_done = (
            sem("arena_zero"), sem("rT_ready"), sem("racc_done"), sem("hnT_ready"), sem("hn_hi_done"), sem("hn_lo_done"))
        xg_done, lg_ready, mask_done, pos_ready, dlog, elog, route_done = (
            sem("xg_done"), sem("lg_ready"), sem("mask_done"), sem("pos_ready"), sem("dlog"),
            sem("elog"), sem("route_done"))
        t_ready, y_zero, gath_ready, comb_ready, pt_ready = (
            sem("t_ready"), sem("y_zero"), sem("gath_ready"),
            sem("comb_ready"), sem("pt_ready"))
        silu_done, mul_done, mTh_done, mTl_done, yh_done, yl_done = (
            sem("silu_done"), sem("mul_done"), sem("mTh_done"), sem("mTl_done"), sem("yh_done"), sem("yl_done"))
        xgh_done, xgl_done, pT_done, gs_done, pick_done, comb_added = (
            sem("xgh_done"), sem("xgl_done"), sem("pT_done"), sem("gs_done"), sem("pick_done"), sem("comb_added"))
        ss_fin, rt_fin, o_done = sem("ss_fin"), sem("rt_fin"), sem("o_done")

        def raw_slot(g):
            return g % RING

        def up_step(s):
            return 0 if s == 0 else 12 * s - 4

        def up_end(s):
            return up_step(s) + 7

        def turn_after(s):
            return 12 * s + 11 if s < STEPS - 1 else PASS_S - 5

        block = ctx.enter_context(nc.Block())

        @block.sync
        def _(sp):
            sp.dma_start(tok[0:N_META, 0, :], meta_tokens).then_inc(tok_in[0], 16)
            sp.dma_start(tok[N_META:P, 0, :], x[0, 0:P - N_META, :]).then_inc(tok_in[0], 16)
            sp.dma_start(tok[:, 1, :], x[0, P - N_META:2 * P - N_META, :]).then_inc(tok_in[1], 16)
            sp.dma_start(tok[0:T - 2 * P, 2, :], x[0, 2 * P - N_META:SEQ, :]).then_inc(tok_in[2], 16)

            def load(g, turns, src, dst_pat, **sizes):
                if g >= RING or not isinstance(turns, int):
                    sp.wait_ge(lo_done, 2 * (g - RING) + 2 + 2 * RING * turns)
                s = raw_slot(g)
                dst = raw[:, s, :].rearrange(dst_pat, **sizes)
                sp.dma_start(dst, src).then_inc(raw_full[s], 16)

            load(0, 0, pool_w[0].rearrange("g (k p) f -> p (g k) f", p=P), "p (a f) -> p a f", f=GW)
            def gate_up(g, turns, col):
                for w in (dense_w_gate, dense_w_up):
                    if g == RING - 2:
                        sp.wait_ge(xT_ready, 6)
                        sp.wait_ge(tn_act, 1)
                        sp.wait_ge(tn_dve, 2)
                    load(g, turns, w[0][:, col].rearrange("(k p) f -> p k f", p=P),
                         "p (k f) -> p k f", k=KD)
                    g += 1
            for n in range(STEPS):
                gate_up(G_GU + 2 * n, 0, slice(256 * n, 256 * n + 256))
            with sp.Fori(1, 2) as it:
                for n in range(STEPS):
                    gate_up(G_GU + 2 * n + 2 * RING, (it - 1) * 2,
                            bass.ds(256 * STEPS * it + 256 * n, 256))
            for n in range(2 * STEPS):
                half, i = divmod(n, STEPS)
                load(G_DN + n, 0, dense_w_down[0, 512 * i:512 * i + 512, 512 * half:512 * half + 512]
                     .rearrange("(k p) f -> p k f", p=P), "p (k f) -> p k f", k=4)
            for n in range(3 * KD // 2):
                j, part = divmod(n, 3)
                col = (1, 2, 0)[part] * D + 256 * j
                load(G_CI + n, 0, conv_w_in[0, :, col:col + 256].rearrange("(k p) f -> p k f", p=P),
                     "p (k f) -> p k f", k=KD)
            for n in range(KD // 2):
                load(G_CO + n, 0, conv_w_out[0, :, 256 * n:256 * n + 256].rearrange("(k p) f -> p k f", p=P),
                     "p (k f) -> p k f", k=KD)

            def expert(t):
                e = t % E
                g = G_MOE

                def turns():
                    return t * (PASS_G // RING)

                def up_like(g, w, s):
                    for h in range(2):
                        load(g + h, turns(), w[0][bass.ds(e, 1), 512 * h:512 * h + 512, 512 * s:512 * s + 512]
                             .rearrange("a (k p) f -> p (a k) f", p=P), "p (k f) -> p k f", k=4)

                def down(g, s):
                    for h in range(2):
                        r = 512 * s + 256 * h
                        load(g + h, turns(), moe_w_down[0][bass.ds(e, 1), r:r + 256, :]
                             .rearrange("a (k p) f -> p (a k) f", p=P), "p (k f) -> p k f", k=2)

                for s in range(STEPS):
                    up_like(g, moe_w_gate, s)
                    up_like(g + 2, moe_w_up, s)
                    g += 4
                    if s >= 1:
                        down(g, s - 1)
                        g += 2
                down(g, STEPS - 1)

            expert(0)
            sp.wait_ge(route_done, 1)
            n_pass = sp.value_load(npass[0:1, 0:1], min_val=E, max_val=2 * E)
            with sp.Fori(1, n_pass) as t:
                expert(t)
            load(G_MOE, n_pass * (PASS_G // RING), moe_w_gate[0, 0, 0:512, 0:512]
                 .rearrange("(k p) f -> p k f", p=P), "p (k f) -> p k f", k=4)
            load(G_MOE + 1, n_pass * (PASS_G // RING), moe_w_gate[0, 0, 512:1024, 0:512]
                 .rearrange("(k p) f -> p k f", p=P), "p (k f) -> p k f", k=4)
            for tt in range(TT):
                sp.wait_ge(o_done, tt + 1)
                sp.dma_start(out[0, tt * P:(tt + 1) * P, :], racc[:, tt, :]).then_inc(out_done, 16)
            sp.wait_ge(out_done, 16 * TT)

        @block.gpsimd
        def _(pool):
            pool.memset(ones[:, :], 1.0).then_inc(consts, 1)
            pool.memset(ident[:, :], 0.0).then_inc(consts, 1)
            pool.memset(eps, EPS).then_inc(consts, 1)
            pool.memset(tss, 1.0).then_inc(consts, 1)
            pool.iota(iota[:, :], pattern=[[1, P]], base=0, channel_multiplier=0,
                      allow_small_or_imprecise_dtypes=True).then_inc(consts, 1)
            pool.memset(slot_of[:, :, :], -1.0).then_inc(consts, 1)
            pool.wait_ge(consts, 6)
            pool.affine_select(out=ident[:, :], in_=ident[:, :], compare_op=ALU.not_equal, fill=1.0,
                               base=0, pattern=[[-1, P]], channel_multiplier=1).then_inc(consts, 1)
            pool.affine_select(out=before[:, :], in_=ones[:, :], compare_op=ALU.is_gt, fill=0.0,
                               base=0, pattern=[[1, P]], channel_multiplier=-1).then_inc(consts, 1)
            made = [0]

            def banded(ins):
                made[0] += 1
                ins.then_inc(bands, 1)

            wide = len(WINDOWS)
            windows = WINDOWS + WINDOWS[-1:]
            for i, w in enumerate(windows):
                banded(pool.memset(band[:, i, :], 1.0 / w))
            assert WINDOWS[-1] == OLD + 2 and WINDOWS[-2] <= OLD
            pool.wait_ge(bands, made[0])
            banded(pool.memset(band[:, wide, OLD:OLD + 1], 1.0 / (OLD + 1)))
            pool.wait_ge(bands, made[0])
            banded(pool.affine_select(out=band[:, :, :], in_=band[:, :, :], compare_op=ALU.is_ge, fill=0.0, base=0,
                                      pattern=[[0, wide + 1], [1, T]], channel_multiplier=-1))
            pool.wait_ge(bands, made[0])
            for i, w in enumerate(windows):
                banded(pool.affine_select(out=band[:, i, :], in_=band[:, i, :], compare_op=ALU.is_ge, fill=0.0, base=w - 1,
                                          pattern=[[-1, T]], channel_multiplier=1))
            pool.wait_ge(bands, made[0])
            for i, w in enumerate(windows):
                banded(pool.affine_select(out=band[:, i, :], in_=band[:, i, :], compare_op=ALU.not_equal, fill=1.0 / w - 1.0,
                                          base=0, pattern=[[1, T]], channel_multiplier=-1))
            pool.wait_ge(bands, made[0])
            banded(pool.affine_select(out=band[:, wide, OLD:OLD + 1], in_=band[:, wide, OLD:OLD + 1], compare_op=ALU.not_equal,
                                      fill=1.0 / (OLD + 1) - 1.0, base=OLD, pattern=[[0, 1]], channel_multiplier=-1))
            assert made[0] == N_BANDS
            pool.wait_ge(sub_done, Q_MOE)
            pool.memset(y_hi[:, :].bitcast(F32), 0.0).then_inc(arena_zero, 1)
            pool.memset(y_lo[:, :].bitcast(F32), 0.0).then_inc(arena_zero, 1)
            pool.memset(pickT[:, :, :].bitcast(F32), 0.0).then_inc(arena_zero, 1)
            pool.memset(slot_gate, 0.0).then_inc(arena_zero, 1)

        @block.scalar
        def _(act):
            act.sem_inc(silu_done, 1)
            act.sem_inc(pT_done, 1)
            prm_src = [(pool_norm, 1), (pool_scale, 1), (dense_norm, 1), (conv_norm, 1), (moe_norm, 1)]
            row = 0
            for src, _ in prm_src:
                act.dma_start(param_rows[row:row + KD, :], src[0].rearrange("(c p) -> c p", p=P)).then_inc(prm_in, 16)
                row += KD
            act.dma_start(param_rows[row:row + TAPS * KD, :],
                          conv_kernel[0].rearrange("t (c p) -> (t c) p", p=P)).then_inc(prm_in, 16)
            act.dma_start(r32[:, :, :], moe_router[0].rearrange("(k p) e -> p k e", p=P)).then_inc(rout_in, 16)

            def hi(q, turns=0):
                if q % 2 == 0:
                    g = q // 2
                    act.wait_ge(raw_full[raw_slot(g)], 16 * (g // RING + 1) + 16 * turns)
                if q >= RING:
                    act.wait_ge(sub_done, q - RING + 1 + 2 * RING * turns)
                nc.scalar.activation(w_hi[:, q % RING, :],
                                     raw[:, raw_slot(q // 2), (q % 2) * SUB:(q % 2 + 1) * SUB],
                                     ACT.Copy).then_inc(hi_done, 1)

            def root(nn, bank, n):
                act.wait_ge(ss_ready, nn)
                nc.scalar.activation(rs[:, 0, 0:n], ps[:, bank, 0:n], ACT.Sqrt, bias=eps,
                                     scale=1.0 / D).then_inc(rt_done, 1)

            def residual_hi(nn, chunks=range(KD)):
                gain = (DN, CN)[nn - 1]
                for c in chunks:
                    act.wait_ge(x_new, KD * (nn - 1) + c + 1)
                    nc.scalar.activation(xn[:, c * T:c * T + NS], X[:, c, OLD:T], ACT.Square).then_inc(sq_done, 1)
                    nc.scalar.activation(n_hi[:, c, :], X[:, c, OLD:T], ACT.Copy,
                                         scale=prm[:, gain + c:gain + c + 1]).then_inc(nh_done, 1)

            act.wait_ge(consts, 8)
            for a, rows in enumerate((P, P, T - 2 * P)):
                act.wait_ge(tok_in[a], 32 if a == 0 else 16)
                nc.scalar.activation(xn[0:rows, 0:D], tok[0:rows, a, :], ACT.Square,
                                     accum_out=tss[0:rows, a:a + 1]).then_inc(tss_done, 1)
                act.wait_ge(tss_done, a + 1)
            nc.scalar.activation(tss, tss, ACT.Sqrt, bias=eps, scale=1.0 / D).then_inc(trt_done, 1)
            act.wait_ge(xT_ready, 1)
            nc.scalar.activation(X[:, 0:4, 0:P], ps[:, 0, :].rearrange("p (k t) -> p k t", k=4), ACT.Copy).then_inc(x_act, 1)
            act.wait_ge(trs_done, 1)
            nc.scalar.activation(tok_n[:, 0, :], tok[:, 0, :], ACT.Copy, scale=tss[:, 0:1]).then_inc(tn_act, 1)
            act.wait_ge(xT_ready, 3)
            nc.scalar.activation(X[:, 0:4, P:2 * P], ps[:, 2, :].rearrange("p (k t) -> p k t", k=4), ACT.Copy).then_inc(x_act, 1)
            act.wait_ge(xT_ready, 5)
            nc.scalar.activation(X[:, :, 2 * P:T], ps[:, 4, 0:KD * (T - 2 * P)].rearrange("p (k t) -> p k t", k=KD),
                                 ACT.Copy).then_inc(x_act, 1)
            hi(0)
            hi(1)
            act.wait_ge(x_dve, 3)
            for c in range(KD):
                act.wait_ge(d_ready, c + 1)
                nc.scalar.activation(n_hi[:, c, :], ps[:, c, 0:NS], ACT.Copy,
                                     scale=prm[:, PN + c:PN + c + 1]).then_inc(nh_done, 1)
            for q in range(2, 2 + LEAD):
                hi(q)
            residual_hi(1)
            root(1, 4, NS)

            sg = xn[:, 0:2 * 2 * NS].rearrange("p (b m t) -> p b m t", b=2, m=2)
            hf = xn[:, 2 * 2 * NS:4 * 2 * NS].rearrange("p (b m t) -> p b m t", b=2, m=2)

            with act.Fori(0, 2) as it:
                for n in range(STEPS):
                    q = 2 * G_GU + 4 * n + LEAD
                    hi(q, 2 * it)
                    hi(q + 1, 2 * it)
                    act.wait_ge(dgate, STEPS * it + n + 1)
                    b = n % 2
                    nc.scalar.activation(sg[:, b], sg[:, b], ACT.Silu).then_inc(dsilu, 1)
                    hi(q + 2, 2 * it)
                    hi(q + 3, 2 * it)
                    act.wait_ge(dmul, 1 + STEPS * it + n + 1)
                    nc.scalar.activation(hid_hi[:, bass.ds(2 * STEPS * it + 2 * n, 2), :], hf[:, b], ACT.Copy).then_inc(dhid_hi, 1)

            q = 2 * G_DN + LEAD
            for _ in range(2 * STEPS):
                hi(q)
                q += 1
            residual_hi(2, range(4))
            for _ in range(2 * STEPS):
                hi(q)
                q += 1
            residual_hi(2, range(4, KD))
            root(2, 7, NS)

            zf = xn[:, 6 * NS:6 * NS + 2 * SEQ].rearrange("p (m t) -> p m t", m=2)
            for j in range(KD // 2):
                hi(q)
                hi(q + 1)
                for i in range(2, 6):
                    hi(q + i)
                q += 6
                act.wait_ge(z_made, j + 1)
                nc.scalar.activation(hid_hi[:, 2 * j:2 * j + 2, 0:SEQ], zf, ACT.Copy).then_inc(z_hi_done, 1)
            while q < Q_MOE + LEAD:
                hi(q)
                q += 1
            for c in range(KD):
                act.wait_ge(x_new, 2 * KD + c + 1)
                nc.scalar.activation(xn[:, c * SEQ:(c + 1) * SEQ], X[:, c, N_META:T], ACT.Square).then_inc(sq_done, 1)
            act.wait_ge(lg_ready, 1)
            nc.scalar.activation(rstd, ps[:, 6, 96:96 + TT], ACT.Sqrt, bias=eps, scale=1.0 / D).then_inc(rt_done, 1)
            for i in range(2 * TT):
                act.wait_ge(rT_ready, i + 1)
                nc.scalar.activation(racc[:, i // 2, 512 * (i % 2):512 * (i % 2) + 512], ps[:, RT_BANK[i], :],
                                     ACT.Copy).then_inc(racc_done, 1)
                if i == 0:
                    act.wait_ge(dlog, 1)
                    nc.scalar.activation(gw[:, 1, :], gw[:, 0, :], ACT.Exp).then_inc(elog, 1)
            for i in range(2 * TT):
                act.wait_ge(hnT_ready, i + 1)
                nc.scalar.activation(hn_hi[:, i // 2, 512 * (i % 2):512 * (i % 2) + 512], ps[:, HT_BANK[i], :],
                                     ACT.Copy, scale=rstd[:, i // 2:i // 2 + 1]).then_inc(hn_hi_done, 1)
            act.wait_ge(hnT_ready, 2 * TT)
            act.dma_start(gfin[:, :], final_norm.rearrange("(a d) -> a d", a=1).to_broadcast([P, D])).then_inc(gfin_in, 16)

            def gathered(t):
                act.wait_ge(gath_ready, t + 1)
                nc.scalar.activation(xg_hi[:, :, :], ps[:, 6:8, :], ACT.Copy).then_inc(xgh_done, 1)

            def y_high(t):
                act.wait_ge(sub_done, Q_MOE + PASS_S * t)
                act.wait_ge(gs_done, 1 + t)
                nc.scalar.activation(y_hi[:, :], ps[:, 4:6, :], ACT.Copy, scale=slot_gate).then_inc(yh_done, 1)

            act.wait_ge(arena_zero, 4)
            act.wait_ge(y_zero, 1)
            gathered(0)
            act.wait_ge(route_done, 1)
            n_pass = act.value_load(npass[0:1, 0:1], min_val=E, max_val=2 * E)
            with act.Fori(0, n_pass) as t:
                turns = t * (PASS_S // (2 * RING))
                for r in range(LEAD, PASS_S + LEAD):
                    if r == 5:
                        y_high(t)
                    for s in range(STEPS):
                        if r == up_step(s) + 4 + BEHIND:
                            act.wait_ge(sub_done, Q_MOE + PASS_S * t + up_step(s) + 4)
                            act.wait_ge(mul_done, 1 + STEPS * t + s)
                            nc.scalar.activation(silu_m[:, :], ps[:, 0, :], ACT.Silu).then_inc(silu_done, 1)
                        if r == turn_after(s) + 1 + BEHIND:
                            act.wait_ge(t_ready, STEPS * t + s + 1)
                            nc.scalar.activation(mT_hi[:, :, :], ps[:, 2, :], ACT.Copy).then_inc(mTh_done, 1)
                    if r == up_end(2) + 1 + BEHIND:
                        act.wait_ge(pt_ready, t + 1)
                        nc.scalar.activation(pickT[:, :, :], ps[:, 3, 0:TT * P], ACT.Copy).then_inc(pT_done, 1)
                    if r == PASS_S + 3:
                        gathered(t + 1)
                    hi(Q_MOE + r, turns)
            y_high(n_pass)
            act.wait_ge(comb_added, TT * n_pass + TT)
            for tt in range(TT):
                nc.scalar.activation(junk[:, :], racc[:, tt, :], ACT.Square, accum_out=ssum[:, tt:tt + 1]).then_inc(ss_fin, 1)
                act.wait_ge(ss_fin, tt + 1)
            nc.scalar.activation(rstd, ssum, ACT.Sqrt, bias=eps, scale=1.0 / D).then_inc(rt_fin, 1)

        @block.vector
        def _(dve):
            dve.sem_inc(dmul, 1)
            dve.sem_inc(dhid_lo, 1)
            dve.sem_inc(mul_done, 1)
            dve.sem_inc(gs_done, 1)
            steps = [0]

            def link(ins):
                steps[0] += 1
                ins.then_inc(dve_step, 1)
                dve.wait_ge(dve_step, steps[0])

            def lo(q, turns=0):
                dve.wait_ge(hi_done, q + 1 + 2 * RING * turns)
                nc.vector.tensor_tensor(w_lo[:, q % RING, :],
                                        raw[:, raw_slot(q // 2), (q % 2) * SUB:(q % 2 + 1) * SUB],
                                        w_hi[:, q % RING, :].bitcast(F32), ALU.subtract).then_inc(lo_done, 1)

            def residual_lo(nn, c):
                gain = (DN, CN)[nn - 1]
                dve.wait_ge(nh_done, KD * nn + c + 1)
                nc.vector.scalar_tensor_tensor(out=n_lo[:, c, :], in0=X[:, c, OLD:T], scalar=prm[:, gain + c:gain + c + 1],
                                               in1=n_hi[:, c, :].bitcast(F32), op0=ALU.mult,
                                               op1=ALU.subtract).then_inc(nl_done, 1)

            def inverse(nn):
                dve.wait_ge(rt_done, nn)
                nc.vector.reciprocal(rs[:, :, :], rs[:, :, :]).then_inc(rs_done, 1)
                dve.wait_ge(rs_done, nn)

            dve.wait_ge(trt_done, 1)
            nc.vector.reciprocal(tss, tss).then_inc(trs_done, 1)
            dve.wait_ge(trs_done, 1)
            nc.vector.tensor_scalar(tok_n[:, 1, :], tok[:, 1, :], tss[:, 1:2], None, ALU.mult).then_inc(tn_dve, 1)
            R = T - 2 * P
            nc.vector.tensor_scalar(tok_n[0:R, 2, :], tok[0:R, 2, :], tss[0:R, 2:3], None, ALU.mult).then_inc(tn_dve, 1)
            dve.wait_ge(xT_ready, 2)
            nc.vector.tensor_copy(X[:, 4:8, 0:P], ps[:, 1, :].rearrange("p (k t) -> p k t", k=4)).then_inc(x_dve, 1)
            dve.wait_ge(xT_ready, 4)
            nc.vector.tensor_copy(X[:, 4:8, P:2 * P], ps[:, 3, :].rearrange("p (k t) -> p k t", k=4)).then_inc(x_dve, 1)
            dve.wait_ge(xT_ready, 6)
            nc.vector.tensor_copy(prm[:, :], ps[:, 6, 0:64]).then_inc(x_dve, 1)
            dve.wait_ge(x_dve, 3)
            lo(0)
            lo(1)
            for c in range(KD):
                dve.wait_ge(nh_done, c + 1)
                nc.vector.scalar_tensor_tensor(out=n_lo[:, c, :], in0=ps[:, c, 0:NS], scalar=prm[:, PN + c:PN + c + 1],
                                               in1=n_hi[:, c, :].bitcast(F32), op0=ALU.mult,
                                               op1=ALU.subtract).then_inc(nl_done, 1)
            for q in range(2, 2 + LEAD):
                lo(q)
            dve.wait_ge(x_act, 3)
            for c in range(KD):
                dve.wait_ge(sub_done, c // 4 + 1)
                nc.vector.scalar_tensor_tensor(out=X[:, c, OLD:T], in0=ps[:, c, 0:NS],
                                               scalar=prm[:, PS + c:PS + c + 1], in1=X[:, c, OLD:T],
                                               op0=ALU.mult, op1=ALU.add).then_inc(x_new, 1)
                if c % 4:
                    residual_lo(1, c - 1)
                if c % 4 == 3:
                    residual_lo(1, c)
            inverse(1)

            sg = xn[:, 0:2 * 2 * NS].rearrange("p (b m t) -> p b m t", b=2, m=2)
            hf = xn[:, 2 * 2 * NS:4 * 2 * NS].rearrange("p (b m t) -> p b m t", b=2, m=2)
            rs_m = rs[:, :, :].to_broadcast([P, 2, NS])
            with dve.Fori(0, 2) as it:
                for n in range(STEPS):
                    q = 2 * G_GU + 4 * n + LEAD
                    b = n % 2
                    lo(q, 2 * it)
                    lo(q + 1, 2 * it)
                    dve.wait_ge(dhid_lo, 1 + STEPS * it + (n - 1 if n >= 2 else 0))
                    dve.wait_ge(sub_done, 2 * G_GU + 4 * (STEPS * it + n) + 2)
                    nc.vector.tensor_tensor(sg[:, b], ps[:, 4 * b:4 * b + 2, 0:NS], rs_m, ALU.mult).then_inc(dgate, 1)
                    lo(q + 2, 2 * it)
                    dve.wait_ge(sub_done, 2 * G_GU + 4 * (STEPS * it + n) + 4)
                    nc.vector.tensor_tensor(hf[:, b], ps[:, 4 * b + 2:4 * b + 4, 0:NS], rs_m, ALU.mult).then_inc(dup, 1)
                    dve.wait_ge(dsilu, STEPS * it + n + 1)
                    dve.wait_ge(dup, STEPS * it + n + 1)
                    nc.vector.tensor_tensor(hf[:, b], hf[:, b], sg[:, b], ALU.mult).then_inc(dmul, 1)
                    lo(q + 3, 2 * it)
                    dve.wait_ge(dhid_hi, STEPS * it + n + 1)
                    at_ = bass.ds(2 * STEPS * it + 2 * n, 2)
                    nc.vector.tensor_tensor(hid_lo[:, at_, :], hf[:, b], hid_hi[:, at_, :].bitcast(F32),
                                            ALU.subtract).then_inc(dhid_lo, 1)
            q = 2 * G_DN + LEAD
            for half in range(2):
                for _ in range(2 * STEPS):
                    lo(q)
                    q += 1
                for c in range(4 * half, 4 * half + 4):
                    if c % 4 < 3:
                        dve.wait_ge(dn_ready, 3 * half + c % 4 + 1)
                    else:
                        dve.wait_ge(sub_done, 2 * G_DN + 2 * STEPS * (half + 1))
                    nc.vector.tensor_tensor(X[:, c, OLD:T], ps[:, (c + 4) % 8, 0:NS], X[:, c, OLD:T], ALU.add).then_inc(x_new, 1)
                for c in range(4 * half, 4 * half + 4):
                    residual_lo(2, c)
            inverse(2)
            link(nc.vector.tensor_tensor(rs2[:, :, :], rs[:, :, :], rs[:, :, :], ALU.mult))
            rs2_m = rs2[:, :, :].to_broadcast([P, 2, NS])
            rs_out = rs[:, :, TAPS - 1:NS].to_broadcast([P, 2, SEQ])
            cs = xn[:, 0:2 * NS].rearrange("p (m t) -> p m t", m=2)
            u = xn[:, 2 * NS:4 * NS].rearrange("p (m t) -> p m t", m=2)
            y = xn[:, 4 * NS:4 * NS + 2 * SEQ].rearrange("p (m t) -> p m t", m=2)
            zf = xn[:, 6 * NS:6 * NS + 2 * SEQ].rearrange("p (m t) -> p m t", m=2)
            for j in range(KD // 2):
                lo(q)
                lo(q + 1)
                if j:
                    dve.wait_ge(u_made, j)
                dve.wait_ge(sub_done, 2 * G_CI + 6 * j + 2)
                nc.vector.tensor_tensor(cs, ps[:, 0:2, 0:NS], rs2_m, ALU.mult).then_inc(c_taken, 1)
                lo(q + 2)
                lo(q + 3)
                dve.wait_ge(c_taken, j + 1)
                dve.wait_ge(sub_done, 2 * G_CI + 6 * j + 4)
                ins = nc.vector.tensor_tensor(u, cs, ps[:, 2:4, 0:NS], ALU.mult)
                ins.then_inc(u_made, 1)
                dve.wait_ge(u_made, j + 1)
                if j:
                    dve.wait_ge(z_made, j)
                for m in range(2):
                    for k in range(TAPS):
                        tap = prm[:, CK + KD * k + 2 * j + m:CK + KD * k + 2 * j + m + 1]
                        if k == 0:
                            link(nc.vector.tensor_scalar(y[:, m], u[:, m, 0:SEQ], tap, None, ALU.mult))
                        else:
                            link(nc.vector.scalar_tensor_tensor(out=y[:, m], in0=u[:, m, k:k + SEQ], scalar=tap,
                                                                in1=y[:, m], op0=ALU.mult, op1=ALU.add))
                lo(q + 4)
                lo(q + 5)
                q += 6
                link(nc.vector.tensor_tensor(y, y, rs_out, ALU.mult))
                dve.wait_ge(sub_done, 2 * G_CI + 6 * j + 6)
                if j:
                    dve.wait_ge(z_lo_done, j)
                nc.vector.tensor_tensor(zf, y, ps[:, 4:6, TAPS - 1:NS], ALU.mult).then_inc(z_made, 1)
                dve.wait_ge(z_hi_done, j + 1)
                nc.vector.tensor_tensor(hid_lo[:, 2 * j:2 * j + 2, 0:SEQ], zf,
                                        hid_hi[:, 2 * j:2 * j + 2, 0:SEQ].bitcast(F32), ALU.subtract).then_inc(z_lo_done, 1)
            while q < Q_MOE:
                lo(q)
                q += 1
            for c in range(KD):
                if c % 2 == 0:
                    dve.wait_ge(co_ready, c // 2 + 1)
                else:
                    dve.wait_ge(sub_done, 2 * G_CO + c + 1)
                nc.vector.tensor_tensor(X[:, c, N_META:T], ps[:, (c + 6) % 8, 0:SEQ], X[:, c, N_META:T],
                                        ALU.add).then_inc(x_new, 1)
                dve.wait_ge(x_new, 2 * KD + c + 1)
                nc.vector.tensor_scalar(xg32[:, c, :], X[:, c, N_META:T], prm[:, MN + c:MN + c + 1], None,
                                        ALU.mult).then_inc(xg_done, 1)
                if c >= 4:
                    lo(Q_MOE + c - 4)

            dve.wait_ge(consts, 8)
            dve.wait_ge(rt_done, 3)
            link(nc.vector.reciprocal(rstd, rstd))
            for tt in range(TT):
                link(nc.vector.tensor_scalar(lg[:, tt, :], ps[:, 6, tt * E:(tt + 1) * E], rstd[:, tt:tt + 1], None, ALU.mult))
            for tt in range(TT):
                link(nc.vector.max(mx[:, tt, :], lg[:, tt, :]))
                link(nc.vector.max_index(ix[:, tt, :], mx[:, tt, :], lg[:, tt, :]))
            nc.vector.tensor_tensor(gw[:, 0, :], mx[:, :, 1], mx[:, :, 0], ALU.subtract).then_inc(dlog, 1)
            link(nc.vector.tensor_copy(ixf[:, :, :], ix[:, :, :]))
            for tt in range(TT):
                nc.vector.tensor_scalar(oh1[:, tt, :], iota[:, 0:E], ixf[:, tt, 0:1], None, ALU.is_equal)
                link(nc.vector.tensor_scalar(oh2[:, tt, :], iota[:, 0:E], ixf[:, tt, 1:2], None, ALU.is_equal))
            nc.vector.tensor_tensor(mask[:, :, :], oh1[:, :, :], oh2[:, :, :], ALU.add).then_inc(mask_done, 1)
            dve.wait_ge(elog, 1)
            link(nc.vector.tensor_scalar(gw[:, 2, :], gw[:, 1, :], 1.0, None, ALU.add))
            link(nc.vector.reciprocal(gw[:, 2, :], gw[:, 2, :]))
            link(nc.vector.tensor_tensor(gw[:, 3, :], gw[:, 1, :], gw[:, 2, :], ALU.mult))
            for tt in range(TT):
                link(nc.vector.tensor_scalar(gates[:, tt, :], oh1[:, tt, :], gw[:, 2, tt:tt + 1], None, ALU.mult))
                link(nc.vector.scalar_tensor_tensor(out=gates[:, tt, :], in0=oh2[:, tt, :], scalar=gw[:, 3, tt:tt + 1],
                                                    in1=gates[:, tt, :], op0=ALU.mult, op1=ALU.add))
            dve.wait_ge(mask_done, 1)
            dve.wait_ge(pos_ready, 1)
            link(nc.vector.scalar_tensor_tensor(out=rank[:, :, :], in0=ps[:, 6, 32:32 + TT * E].rearrange("p (a e) -> p a e", a=TT),
                                                scalar=1.0, in1=mask[:, :, :], op0=ALU.add, op1=ALU.mult))
            nc.vector.tensor_scalar(slot_of[:, :, E:2 * E], rank[:, :, :], -1.0 - P, None, ALU.add)
            link(nc.vector.tensor_scalar(slot_of[:, :, 0:E], rank[:, :, :], -1.0, None, ALU.add))

            def make_pick(t):
                for tt in range(TT):
                    ins = nc.vector.tensor_scalar(pick[:, tt, :], iota[:, :], slot_of[:, tt, bass.ds(t, 1)], None,
                                                  ALU.is_equal)
                ins.then_inc(pick_done, 1)

            dve.wait_ge(arena_zero, 4)
            make_pick(0)
            link(nc.vector.tensor_reduce(cmax, ps[:, 6, 64:64 + E], AX_X, ALU.max))
            link(nc.vector.tensor_scalar(cmax, cmax, float(P), float(E), ALU.is_gt, ALU.mult))
            nc.vector.tensor_scalar(npass[:, :], cmax, float(E), None, ALU.add).then_inc(route_done, 1)
            for i in range(2 * TT):
                at_ = slice(512 * (i % 2), 512 * (i % 2) + 512)
                dve.wait_ge(hn_hi_done, i + 1)
                nc.vector.scalar_tensor_tensor(out=hn_lo[:, i // 2, at_], in0=ps[:, HT_BANK[i], :],
                                               scalar=rstd[:, i // 2:i // 2 + 1], in1=hn_hi[:, i // 2, at_].bitcast(F32),
                                               op0=ALU.mult, op1=ALU.subtract).then_inc(hn_lo_done, 1)

            def gathered(t):
                dve.wait_ge(gath_ready, t + 1)
                nc.vector.tensor_copy(xg_lo[:, 0:4, :], ps[:, 3, :].rearrange("p (k t) -> p k t", k=4))
                nc.vector.tensor_copy(xg_lo[:, 4:8, :], ps[:, 0, :].rearrange("p (k t) -> p k t", k=4)).then_inc(xgl_done, 1)

            def y_low(t):
                dve.wait_ge(yh_done, t + 1)
                nc.vector.scalar_tensor_tensor(out=y_lo[:, :], in0=ps[:, 4:6, :].rearrange("p a n -> p (a n)"), scalar=slot_gate,
                                               in1=y_hi[:, :].bitcast(F32), op0=ALU.mult,
                                               op1=ALU.subtract).then_inc(yl_done, 1)

            def combined(t):
                for tt in range(TT):
                    b = (6, 2)[tt]
                    dve.wait_ge(comb_ready, TT * t + tt + 1)
                    nc.vector.tensor_tensor(racc[:, tt, :], ps[:, b:b + 2, :].rearrange("p a n -> p (a n)"),
                                            racc[:, tt, :], ALU.add).then_inc(comb_added, 1)

            gathered(0)
            dve.wait_ge(route_done, 1)
            n_pass = dve.value_load(npass[0:1, 0:1], min_val=E, max_val=2 * E)
            with dve.Fori(0, n_pass) as t:
                turns = t * (PASS_S // (2 * RING))
                for r in range(LEAD, PASS_S + LEAD):
                    if r == 5:
                        y_low(t)
                    if r == 11:
                        combined(t)
                    for s in range(STEPS):
                        if r == up_end(s) + BEHIND:
                            dve.wait_ge(silu_done, 1 + STEPS * t + s + 1)
                            dve.wait_ge(sub_done, Q_MOE + PASS_S * t + up_end(s) + 1)
                            nc.vector.tensor_tensor(hid_m[:, :], silu_m[:, :], ps[:, 1, :], ALU.mult).then_inc(mul_done, 1)
                        if r == turn_after(s) + BEHIND:
                            dve.wait_ge(mTh_done, STEPS * t + s + 1)
                            nc.vector.tensor_tensor(mT_lo[:, :, :], ps[:, 2, :].rearrange("p (k t) -> p k t", k=4),
                                                    mT_hi[:, :, :].bitcast(F32), ALU.subtract).then_inc(mTl_done, 1)
                    if r == up_end(2) + BEHIND:
                        dve.wait_ge(pT_done, 1 + t + 1)
                        nc.vector.tensor_copy(slot_gate, ps[:, 3, TT * P:TT * P + 1]).then_inc(gs_done, 1)
                        make_pick(t + 1)
                    if r == PASS_S + 2:
                        gathered(t + 1)
                    lo(Q_MOE + r, turns)
            y_low(n_pass)
            combined(n_pass)
            dve.wait_ge(rt_fin, 1)
            dve.wait_ge(gfin_in, 16)
            link(nc.vector.reciprocal(rstd, rstd))
            for tt in range(TT):
                nc.vector.scalar_tensor_tensor(out=racc[:, tt, :], in0=racc[:, tt, :], scalar=rstd[:, tt:tt + 1],
                                               in1=gfin[:, :], op0=ALU.mult, op1=ALU.mult).then_inc(o_done, 1)

        @block.tensor
        def _(pe):
            mm = nc.tensor.matmul

            def use(q, turns=0):
                pe.wait_ge(lo_done, q + 1 + 2 * RING * turns)

            def features(bank, n, sub_col, q, mov_hi, mov_lo, first, last):
                wh = w_hi[:, q % RING, sub_col:sub_col + P]
                wl = w_lo[:, q % RING, sub_col:sub_col + P]
                mm(ps[:, bank, 0:n], wh, mov_hi, start=first, stop=False)
                mm(ps[:, bank, 0:n], wh, mov_lo, start=False, stop=False)
                return mm(ps[:, bank, 0:n], wl, mov_hi, start=False, stop=last)

            def mean_square(nn, bank):
                for c in range(KD):
                    pe.wait_ge(sq_done, KD * (nn - 1) + c + 1)
                    last = mm(ps[:, bank, 0:NS], ones[:, :], xn[:, c * T:c * T + NS], start=(c == 0), stop=(c == KD - 1))
                last.then_inc(ss_ready, 1)

            pe.wait_ge(consts, 8)
            for a in range(2):
                pe.wait_ge(tok_in[a], 32 if a == 0 else 16)
                for h in range(2):
                    for k in range(4):
                        c = 4 * h + k
                        last = nc.tensor.transpose(ps[:, 2 * a + h, k * P:(k + 1) * P], tok[:, a, c * P:(c + 1) * P], ident[:, :])
                    last.then_inc(xT_ready, 1)
            R = T - 2 * P
            pe.wait_ge(tok_in[2], 16)
            for c in range(KD):
                last = nc.tensor.transpose(ps[:, 4, c * R:(c + 1) * R], tok[0:R, 2, c * P:(c + 1) * P], ident[0:R, 0:R])
            last.then_inc(xT_ready, 1)
            pe.wait_ge(prm_in, 16 * 6)
            nc.tensor.transpose(ps[:, 6, 0:64], param_rows[:, :], ident[0:64, 0:64]).then_inc(xT_ready, 1)
            pe.wait_ge(tn_act, 1)
            pe.wait_ge(tn_dve, 2)
            pe.wait_ge(bands, N_BANDS)
            pe.wait_ge(x_act, 3)
            pe.wait_ge(x_dve, 3)
            for c in range(KD):
                g = c * P // GW
                f = slice(c * P, (c + 1) * P)
                mm(ps[:, c, 0:NS], tok_n[:, 0, f], band[:, g + (g == len(WINDOWS) - 1), OLD:T], start=True, stop=False)
                mm(ps[:, c, P - OLD:NS], tok_n[:, 1, f], band[:, g, 0:T - P], start=False, stop=False)
                mm(ps[:, c, 2 * P - OLD:NS], tok_n[0:R, 2, f], band[0:R, g, 0:R], start=False, stop=True).then_inc(d_ready, 1)

            for g in range(GROUPS):
                q = g // 2
                use(q)
                for m in range(2):
                    for k in range(2):
                        c = 2 * g + k
                        pe.wait_ge(nl_done, 2 * g + 2)
                        last = features(2 * g + m, NS, (g % 2) * 2 * GW + k * GW + m * P, q,
                                        n_hi[:, c, :], n_lo[:, c, :], k == 0, k == 1)
                if g % 2:
                    last.then_inc(sub_done, 1)

            pe.wait_ge(x_new, 5)
            mean_square(1, 4)

            with pe.Fori(0, 2) as it:
                for n in range(STEPS):
                    q = 2 * G_GU + 4 * n
                    b = 4 * (n % 2)
                    pe.wait_ge(dmul, 1 + STEPS * it + (n - 1 if n >= 2 else 0))
                    if n == 1:
                        pe.wait_ge(rt_done, 1)
                    for part in range(2):
                        for s in range(2):
                            use(q, 2 * it)
                            for m in range(2):
                                for k in range(4):
                                    c = 4 * s + k
                                    if n == 0 and part == 0:
                                        pe.wait_ge(nl_done, KD + c + 1)
                                    last = features(b + 2 * part + m, NS, k * 256 + m * P, q, n_hi[:, c, :], n_lo[:, c, :],
                                                    c == 0, c == KD - 1)
                            last.then_inc(sub_done, 1)
                            q += 1
            q = 2 * G_DN
            for half in range(2):
                pe.wait_ge(dmul, 1 + 2 * STEPS - 1 + half)
                for i in range(2 * STEPS):
                    use(q)
                    if half == 0:
                        pe.wait_ge(dhid_lo, 1 + i + 1)
                    for c in range(4):
                        for k in range(2):
                            f = 2 * i + k
                            last = features((4 * half + c + 4) % 8, NS, k * 512 + c * P, q, hid_hi[:, f, :], hid_lo[:, f, :],
                                            f == 0, f == KF - 1)
                        if i == 2 * STEPS - 1 and c < 3:
                            last.then_inc(dn_ready, 1)
                    last.then_inc(sub_done, 1)
                    q += 1
            pe.wait_ge(x_new, KD + 4)
            mean_square(2, 7)
            for j in range(KD // 2):
                for part in range(3):
                    for s in range(2):
                        use(q)
                        if j and s == 0:
                            pe.wait_ge((c_taken, u_made, z_made)[part], j)
                        for m in range(2):
                            for k in range(4):
                                c = 4 * s + k
                                if j == 0 and part == 0 and m == 0:
                                    pe.wait_ge(nl_done, 2 * KD + c + 1)
                                last = features(2 * part + m, NS, k * 256 + m * P, q, n_hi[:, c, :], n_lo[:, c, :],
                                                c == 0, c == KD - 1)
                        last.then_inc(sub_done, 1)
                        q += 1
            for i in range(KD // 2):
                if i == 1:
                    pe.wait_ge(z_made, KD // 2)
                for s in range(2):
                    use(q)
                    for m in range(2):
                        for k in range(4):
                            c = 4 * s + k
                            if i == 0 and m == 0:
                                pe.wait_ge(z_lo_done, c // 2 + 1)
                            last = features((2 * i + m + 6) % 8, SEQ, k * 256 + m * P, q, hid_hi[:, c, 0:SEQ],
                                            hid_lo[:, c, 0:SEQ], c == 0, c == KD - 1)
                        if s == 1 and m == 0:
                            last.then_inc(co_ready, 1)
                    last.then_inc(sub_done, 1)
                    q += 1
            pe.wait_ge(rout_in, 16)
            for tt in range(TT):
                for c in range(KD):
                    pe.wait_ge(sq_done, 2 * KD + c + 1)
                    mm(ps[:, 6, 96 + tt:97 + tt], xn[:, c * SEQ + tt * P:c * SEQ + (tt + 1) * P], ones[:, 0:1],
                       start=(c == 0), stop=(c == KD - 1))
            for tt in range(TT):
                for c in range(KD):
                    pe.wait_ge(xg_done, c + 1)
                    last = mm(ps[:, 6, tt * E:(tt + 1) * E], xg32[:, c, tt * P:(tt + 1) * P], r32[:, c, :],
                              start=(c == 0), stop=(c == KD - 1))
            last.then_inc(lg_ready, 1)

            def turn(src, first, i, bank, ready):
                tt, h = divmod(i, 2)
                for k in range(4):
                    col = first + tt * P
                    last = nc.tensor.transpose(ps[:, bank, k * P:(k + 1) * P], src[:, 4 * h + k, col:col + P], ident[:, :])
                last.then_inc(ready, 1)

            for i in range(2 * TT):
                turn(X, N_META, i, RT_BANK[i], rT_ready)
            for i in range(2 * TT):
                if HT_BANK[i] == RT_BANK[0]:
                    pe.wait_ge(racc_done, 1)
                turn(xg32, 0, i, HT_BANK[i], hnT_ready)
            pe.wait_ge(mask_done, 1)
            for tt in range(TT):
                o = ps[:, 6, 32 + tt * E:32 + (tt + 1) * E]
                for s in range(tt):
                    mm(o, ones[:, :], mask[:, s, :], start=(s == 0), stop=False)
                mm(o, before[:, :], mask[:, tt, :], start=(tt == 0), stop=True)
            for tt in range(TT):
                last = mm(ps[:, 6, 64:64 + E], ones[:, :], mask[:, tt, :], start=(tt == 0), stop=(tt == TT - 1))
            last.then_inc(pos_ready, 1)
            pe.wait_ge(arena_zero, 4)
            pe.wait_ge(racc_done, 4)
            pe.wait_ge(hn_lo_done, 4)
            for h in range(2):
                last = mm(ps[:, 4 + h, :], y_hi[:, 0:P], y_lo[:, 0:512], start=True, stop=True)
            last.then_inc(y_zero, 1)

            def gather(t):
                for src, banks in ((hn_hi, (6, 7)), (hn_lo, (3, 0))):
                    for c in range(KD):
                        for tt in range(TT):
                            last = mm(ps[:, banks[c // 4], (c % 4) * P:(c % 4 + 1) * P], src[:, tt, c * P:(c + 1) * P],
                                      pick[:, tt, :], start=(tt == 0), stop=(tt == TT - 1))
                last.then_inc(gath_ready, 1)

            def combine(t):
                pe.wait_ge(yl_done, t + 1)
                pe.wait_ge(pT_done, 1 + t)
                for tt in range(TT):
                    for h in range(2):
                        o = ps[:, (6, 2)[tt] + h, :]
                        mm(o, pickT[:, tt, :], y_hi[:, 512 * h:512 * h + 512], start=True, stop=False)
                        last = mm(o, pickT[:, tt, :], y_lo[:, 512 * h:512 * h + 512], start=False, stop=True)
                    last.then_inc(comb_ready, 1)

            def stream(bank, q, turns, piece, k, tok_hi, tok_lo, first, last_one):
                o = ps[:, bank, :]
                wh = w_hi[:, q % RING, piece * 512:piece * 512 + 512]
                wl = w_lo[:, q % RING, piece * 512:piece * 512 + 512]
                mm(o, tok_hi, wh, start=first, stop=False)
                mm(o, tok_hi, wl, start=False, stop=False)
                return mm(o, tok_lo, wh, start=False, stop=last_one)

            pe.wait_ge(pick_done, 1)
            pe.wait_ge(route_done, 1)
            gather(0)
            n_pass = pe.value_load(npass[0:1, 0:1], min_val=E, max_val=2 * E)
            with pe.Fori(0, n_pass) as t:
                turns = t * (PASS_S // (2 * RING))
                r = 0

                def up_like(bank):
                    nonlocal r
                    for i in range(4):
                        q = Q_MOE + r
                        use(q, turns)
                        for k in range(2):
                            c = 2 * i + k
                            last = stream(bank, q, turns, k, k, xg_hi[:, c, :], xg_lo[:, c, :], c == 0, c == KD - 1)
                        last.then_inc(sub_done, 1)
                        r += 1

                def turn_hidden(s):
                    pe.wait_ge(mul_done, 1 + STEPS * t + s + 1)
                    if s == 0:
                        pe.wait_ge(comb_added, TT * t + TT)
                    for k in range(4):
                        last = nc.tensor.transpose(ps[:, 2, k * P:(k + 1) * P], hid_m[:, k * P:(k + 1) * P], ident[:, :])
                    last.then_inc(t_ready, 1)

                def down(s):
                    nonlocal r
                    pe.wait_ge(mTl_done, STEPS * t + s + 1)
                    for k in range(4):
                        q = Q_MOE + r
                        use(q, turns)
                        for h in range(2):
                            last = stream(4 + h, q, turns, h, k, mT_hi[:, k, :], mT_lo[:, k, :], s == 0 and k == 0,
                                          s == STEPS - 1 and k == 3)
                        last.then_inc(sub_done, 1)
                        r += 1

                for s in range(STEPS):
                    if s == 0:
                        pe.wait_ge(xgh_done, t + 1)
                        pe.wait_ge(xgl_done, t + 1)
                    pe.wait_ge(silu_done, 1 + STEPS * t + s)
                    up_like(0)
                    if s >= 1:
                        turn_hidden(s - 1)
                    pe.wait_ge(mul_done, 1 + STEPS * t + s)
                    up_like(1)
                    if s == 0:
                        combine(t)
                    if s == 2:
                        pe.wait_ge(comb_added, TT * t + TT)
                        for tt in range(TT):
                            nc.tensor.transpose(ps[:, 3, tt * P:(tt + 1) * P], pick[:, tt, :].bitcast(F32), ident[:, :])
                        for tt in range(TT):
                            last = mm(ps[:, 3, TT * P:TT * P + 1], pick[:, tt, :].bitcast(F32),
                                      gates[:, tt, bass.ds(t % E, 1)], start=(tt == 0), stop=(tt == TT - 1))
                        last.then_inc(pt_ready, 1)
                    if s >= 1:
                        down(s - 1)
                pe.wait_ge(pick_done, t + 2)
                pe.wait_ge(pT_done, 1 + t + 1)
                pe.wait_ge(gs_done, 1 + t + 1)
                pe.wait_ge(silu_done, 1 + STEPS * t + STEPS)
                gather(t + 1)
                turn_hidden(STEPS - 1)
                down(STEPS - 1)
            combine(n_pass)


_INS = ["x", "meta_tokens", "pool_norm", "pool_w", "pool_scale", "dense_norm", "dense_w_gate", "dense_w_up",
        "dense_w_down", "conv_norm", "conv_w_in", "conv_kernel", "conv_w_out", "moe_norm", "moe_router",
        "moe_w_gate", "moe_w_up", "moe_w_down", "final_norm"]


def kernel(**inputs):
    import numpy as np
    import concourse.bacc as bacc
    from concourse import mybir as mb
    from concourse.bass_utils import run_bass_kernel_spmd

    nc = bacc.Bacc("TRN2", target_bir_lowering=False, num_devices=1)
    arrays, args = {}, []
    for name in _INS:
        a = np.ascontiguousarray(inputs[name])
        arrays[name] = a
        args.append(nc.dram_tensor(name, a.shape, mb.dt.from_np(a.dtype), kind="ExternalInput").ap())
    o = nc.dram_tensor("out", arrays["x"].shape, mb.dt.from_np(arrays["x"].dtype), kind="ExternalOutput").ap()
    build_encoder(nc, *args, o)
    r = run_bass_kernel_spmd(nc, [arrays], core_ids=[0])
    return r.results[0]["out"]
```

```python
from contextlib import ExitStack

import concourse.bass as bass
from concourse import mybir

ACT = mybir.ActivationFunctionType
ALU = mybir.AluOpType
AX_X = mybir.AxisListType.X
F32 = mybir.dt.float32
F32R = mybir.dt.float32r
I32 = mybir.dt.int32
U32 = mybir.dt.uint32

P = 128


def build_encoder(nc, x, meta_tokens, pool_norm, pool_w, pool_scale, dense_norm, dense_w_gate,
                  dense_w_up, dense_w_down, conv_norm, conv_w_in, conv_kernel, conv_w_out,
                  moe_norm, moe_router, moe_w_gate, moe_w_up, moe_w_down, final_norm, out):
    SEQ, D = x.shape[1], x.shape[2]
    N_META = meta_tokens.shape[0]
    T = SEQ + N_META
    F = dense_w_gate.shape[2]
    E = moe_router.shape[2]
    TAPS = conv_kernel.shape[1]
    GROUPS, GW = pool_w.shape[1], pool_w.shape[2]
    WINDOWS = (2, 4, 8, 16)
    EPS = 1e-6
    KD = D // P
    KF = F // P
    NS = SEQ + TAPS - 1
    OLD = T - NS
    TT = SEQ // P
    STEPS = F // 512
    assert (KD, TT, GW, GROUPS, E, KF, STEPS, TAPS) == (8, 2, 256, 4, 8, 28, 7, 3)

    RING = 7
    GRAN, SUB = 2048, 1024
    G_GU = 1
    G_DN = G_GU + 2 * KF // 2
    G_CI = G_DN + KF // 2
    G_CO = G_CI + 3 * D // 256
    G_MOE = G_CO + D // 256
    PASS_G = 6 * STEPS
    PASS_S = 2 * PASS_G
    Q_MOE = 2 * G_MOE
    LEAD = 4
    M_LEAD = 2
    N_BANDS = 3 * len(WINDOWS) + 6
    BEHIND = 5
    assert PASS_S % RING == 0 and KF % RING == 0

    SPARE = 3
    ring_order = [(G_MOE + i) % RING for i in range(RING)]
    expert_slot = ring_order + [RING + i for i in range(SPARE)]
    while len(expert_slot) < PASS_G:
        expert_slot += ring_order + [RING + len(expert_slot) // RING % SPARE]
    assert len(expert_slot) == PASS_G

    def expert_granule(q):
        ahead, r = divmod(q - 2 * G_MOE, PASS_S)
        return r // 2, ahead

    with ExitStack() as ctx:
        def sem(name):
            return ctx.enter_context(nc.semaphore(name))

        base = (nc.sbuf_base + 63) // 64 * 64
        at = [base]

        def region(nbytes):
            a = at[0]
            at[0] += (nbytes + 31) // 32 * 32
            return a

        def place(name, addr, shape, dt):
            return nc.alloc_sbuf_tensor_at(name, shape, dt, offset=addr)

        A_RAW, A_HI, A_LO = region(RING * GRAN * 4), region(RING * SUB * 4), region(RING * SUB * 4)
        A_AH, A_AL = region(KF * NS * 4), region(KF * NS * 4)
        A_NH, A_NL = region(KD * NS * 4), region(KD * NS * 4)
        A_XN, A_X = region(KD * T * 4), region(KD * T * 4)

        raw = [place(f"raw{i}", A_RAW + i * GRAN * 4, [P, GRAN], F32) for i in range(RING)]
        raw += [place(f"raw{RING + i}", a, [P, GRAN], F32)
                for i, a in enumerate((A_AH + 20480, A_AL + 20480, A_X))]
        w_hi = place("w_hi", A_HI, [P, RING, SUB], F32R)
        w_lo = place("w_lo", A_LO, [P, RING, SUB], F32R)
        X = place("X", A_X, [P, KD, T], F32)
        xn = place("xn", A_XN, [P, KD * T], F32)
        xn_sq = place("xn_sq", A_NL, [P, KD, SEQ], F32)
        n_hi = place("n_hi", A_NH, [P, KD, NS], F32R)
        n_lo = place("n_lo", A_NL, [P, KD, NS], F32R)
        hid_hi = place("hid_hi", A_AH, [P, KF, NS], F32R)
        hid_lo = place("hid_lo", A_AL, [P, KF, NS], F32R)
        param_rows = place("param_rows", A_AL, [64, P], F32)
        tok = place("tok", A_RAW + 5 * GRAN * 4, [P, 3, D], F32)
        tok_n = place("tok_n", A_AL + 512, [P, 3, D], F32)
        band = place("band", A_AH, [P, len(WINDOWS) + 1, T], F32)
        hn_hi = place("hn_hi", A_AH, [P, TT, D], F32R)
        hn_lo = place("hn_lo", A_AL, [P, TT, D], F32R)
        xg_hi = place("xg_hi", A_AH + 8192, [P, KD, P], F32R)
        xg_lo = place("xg_lo", A_AL + 8192, [P, KD, P], F32R)
        mT_hi = place("mT_hi", A_AH + 12288, [P, 4, P], F32R)
        mT_lo = place("mT_lo", A_AL + 12288, [P, 4, P], F32R)
        y_hi = place("y_hi", A_AH + 14336, [P, D], F32R)
        y_lo = place("y_lo", A_AL + 14336, [P, D], F32R)
        pick = place("pick", A_AH + 18432, [P, TT, P], F32R)
        pickT = place("pickT", A_AH + 19456, [P, TT, P], F32R)
        xg32 = place("xg32", A_NH, [P, KD, SEQ], F32)
        racc = place("racc", A_XN, [P, TT, D], F32)
        gfin = place("gfin", A_NH, [P, D], F32)
        silu_m = place("silu_m", A_NL, [P, 512], F32)
        hid_m = place("hid_m", A_NL + 2048, [P, 512], F32)
        junk = place("junk", A_NH + 4096, [P, D], F32)

        ident = place("ident", region(512), [P, P], F32)
        ones = place("ones", region(512), [P, P], F32)
        before = place("before", region(512), [P, P], F32)
        iota = place("iota", region(512), [P, P], F32)
        prm = place("prm", region(256), [P, 64], F32)
        r32 = place("r32", region(256), [P, KD, E], F32)
        rs = place("rs", region(4 * NS), [P, 1, NS], F32)
        rs2 = place("rs2", region(4 * NS), [P, 1, NS], F32)
        ssq = rs2
        lg = place("lg", region(64), [P, TT, E], F32)
        mx = place("mx", region(64), [P, TT, E], F32)
        ix = place("ix", region(64), [P, TT, E], U32)
        ixf = place("ixf", region(64), [P, TT, E], F32)
        oh1 = place("oh1", region(64), [P, TT, E], F32)
        oh2 = place("oh2", region(64), [P, TT, E], F32)
        mask = place("mask", region(64), [P, TT, E], F32)
        gates = place("gates", region(64), [P, TT, E], F32)
        slot_of = place("slot_of", region(160), [P, TT, 20], F32)
        rank = place("rank", region(64), [P, TT, E], F32)
        gw = place("gw", region(64), [P, 4, TT], F32)
        small = place("small", region(64), [P, 16], F32)
        npass = place("npass", region(32), [P, 1], I32)
        assert at[0] <= nc.sbuf_usable_end, at[0] - nc.sbuf_usable_end
        eps, cmax, ssum, rstd, slot_gate, tss, warm = (small[:, 0:1], small[:, 1:2], small[:, 2:4],
                                                 small[:, 4:6], small[:, 6:7], small[:, 8:11], small[:, 12:14])
        ps = ctx.enter_context(nc.psum_tensor("ps", [P, 8, 512], F32))

        TURNS = ((0, 0), (1, 0), (0, 1), (1, 1))
        RT_BANK, HT_BANK = (0, 1, 4, 5), (2, 3, 0, 1)
        PN, PS, DN, CN, MN, CK = 0, KD, 2 * KD, 3 * KD, 4 * KD, 5 * KD

        tok_in = [sem(f"tok_in{i}") for i in range(3)]
        raw_full = [sem(f"raw_full{i}") for i in range(RING + SPARE)]
        hi_done = sem("hi_done")
        lo_done = sem("lo_done")
        sub_done = sem("sub_done")
        param_in = sem("param_in")
        router_in = sem("router_in")
        final_in = sem("final_in")
        out_done = sem("out_done")
        consts = sem("consts")
        bands = sem("bands")
        tok_squared = sem("tok_squared")
        tok_root = sem("tok_root")
        tok_inverse = sem("tok_inverse")
        tok_n_act = sem("tok_n_act")
        tok_n_dve = sem("tok_n_dve")
        tok_turned = sem("tok_turned")
        x_act = sem("x_act")
        x_dve = sem("x_dve")
        d_ready = sem("d_ready")
        x_new = sem("x_new")
        sq_done = sem("sq_done")
        sum_done = sem("sum_done")
        ss_ready = sem("ss_ready")
        root_done = sem("root_done")
        inverse_done = sem("inverse_done")
        n_hi_done = sem("n_hi_done")
        n_lo_done = sem("n_lo_done")
        gate_normed = sem("gate_normed")
        up_normed = sem("up_normed")
        gate_silu = sem("gate_silu")
        dense_mul = sem("dense_mul")
        dense_hi = sem("dense_hi")
        dense_lo = sem("dense_lo")
        down_ready = sem("down_ready")
        c_taken = sem("c_taken")
        u_made = sem("u_made")
        z_made = sem("z_made")
        z_hi_done = sem("z_hi_done")
        z_lo_done = sem("z_lo_done")
        conv_ready = sem("conv_ready")
        xg32_done = sem("xg32_done")
        lg_ready = sem("lg_ready")
        rstd_done = sem("rstd_done")
        mask_done = sem("mask_done")
        pos_ready = sem("pos_ready")
        count_ready = sem("count_ready")
        logit_gap = sem("logit_gap")
        gap_exp = sem("gap_exp")
        gates_done = sem("gates_done")
        route_done = sem("route_done")
        racc_turned = sem("racc_turned")
        racc_done = sem("racc_done")
        hn_turned = sem("hn_turned")
        hn_hi_done = sem("hn_hi_done")
        hn_lo_done = sem("hn_lo_done")
        arena_zero = sem("arena_zero")
        pick_done = sem("pick_done")
        gath_ready = sem("gath_ready")
        xg_hi_done = sem("xg_hi_done")
        xg_lo_done = sem("xg_lo_done")
        silu_done = sem("silu_done")
        mul_done = sem("mul_done")
        hid_turned = sem("hid_turned")
        mT_hi_done = sem("mT_hi_done")
        mT_lo_done = sem("mT_lo_done")
        pickT_ready = sem("pickT_ready")
        pickT_done = sem("pickT_done")
        slot_gate_done = sem("slot_gate_done")
        y_hi_done = sem("y_hi_done")
        y_lo_done = sem("y_lo_done")
        comb_ready = sem("comb_ready")
        comb_added = sem("comb_added")
        out_squared = sem("out_squared")
        out_root = sem("out_root")
        out_ready = sem("out_ready")
        dve_step = sem("dve_step")

        def raw_slot(q):
            return q // 2 % RING if q < Q_MOE else expert_slot[expert_granule(q)[0]]

        def raw_sub(q):
            return raw[raw_slot(q)][:, (q % 2) * SUB:(q % 2 + 1) * SUB]

        def loaded(q, turns, t):
            if q < Q_MOE:
                return 16 * (q // 2 // RING + 1) + 16 * turns
            slot, (j, ahead) = raw_slot(q), expert_granule(q)
            dense = len([g for g in range(G_MOE) if g % RING == slot])
            a_pass = expert_slot.count(slot)
            return 16 * (dense + a_pass * ahead + expert_slot[:j + 1].count(slot)) + 16 * a_pass * t

        def up_step(s):
            return 0 if s == 0 else 12 * s - 4

        def up_end(s):
            return up_step(s) + 7

        def turn_after(s):
            return 12 * s + 11 if s < STEPS - 1 else PASS_S - 5

        block = ctx.enter_context(nc.Block())

        @block.sync
        def _(sp):
            sp.dma_start(tok[0:N_META, 0, :], meta_tokens).then_inc(tok_in[0], 16)
            sp.dma_start(tok[N_META:P, 0, :], x[0, 0:P - N_META, :]).then_inc(tok_in[0], 16)
            sp.dma_start(tok[:, 1, :], x[0, P - N_META:2 * P - N_META, :]).then_inc(tok_in[1], 16)
            sp.dma_start(tok[0:T - 2 * P, 2, :], x[0, 2 * P - N_META:SEQ, :]).then_inc(tok_in[2], 16)

            def load(g, src, dst_pat, **sizes):
                if g >= RING:
                    sp.wait_ge(lo_done, 2 * (g - RING) + 2)
                fill(g % RING, src, dst_pat, **sizes)

            def fill(slot, src, dst_pat, **sizes):
                sp.dma_start(raw[slot][:, :].rearrange(dst_pat, **sizes), src).then_inc(raw_full[slot], 16)

            def slot_free(j, t):
                slot = expert_slot[j]
                before_j = [i for i in range(j) if expert_slot[i] == slot]
                if before_j:
                    sp.wait_ge(lo_done, Q_MOE + 2 * before_j[-1] + 2 + PASS_S * t)
                elif not isinstance(t, int):
                    last = [i for i in range(PASS_G) if expert_slot[i] == slot][-1]
                    sp.wait_ge(lo_done, Q_MOE + 2 * last + 2 - PASS_S + PASS_S * t)
                elif slot < RING:
                    sp.wait_ge(lo_done, 2 * (G_MOE + j - RING) + 2)
                elif slot < RING + SPARE - 1:
                    sp.wait_ge(sub_done, 2 * G_CI)
                else:
                    sp.wait_ge(racc_turned, 2 * TT)

            prm_src = [(pool_norm, 1), (pool_scale, 1), (dense_norm, 1), (conv_norm, 1), (moe_norm, 1)]
            row = 0
            for src, _ in prm_src:
                sp.dma_start(param_rows[row:row + KD, :], src[0].rearrange("(c p) -> c p", p=P)).then_inc(param_in, 16)
                row += KD
            sp.dma_start(param_rows[row:row + TAPS * KD, :],
                          conv_kernel[0].rearrange("t (c p) -> (t c) p", p=P)).then_inc(param_in, 16)
            sp.dma_start(r32[:, :, :], moe_router[0].rearrange("(k p) e -> p k e", p=P)).then_inc(router_in, 16)

            load(0, pool_w[0].rearrange("g (k p) f -> p (g k) f", p=P), "p (a f) -> p a f", f=GW)
            def gate_up(g, col):
                for w in (dense_w_gate, dense_w_up):
                    if g == RING - 2:
                        sp.wait_ge(tok_turned, 6)
                        sp.wait_ge(tok_n_act, 1)
                        sp.wait_ge(tok_n_dve, 2)
                    load(g, w[0][:, col].rearrange("(k p) f -> p k f", p=P),
                         "p (k f) -> p k f", k=KD)
                    g += 1
            for n in range(2 * STEPS):
                gate_up(G_GU + 2 * n, slice(256 * n, 256 * n + 256))
            for n in range(2 * STEPS):
                half, i = divmod(n, STEPS)
                load(G_DN + n, dense_w_down[0, 512 * i:512 * i + 512, 512 * half:512 * half + 512]
                     .rearrange("(k p) f -> p k f", p=P), "p (k f) -> p k f", k=4)
            for n in range(3 * KD // 2):
                j, part = divmod(n, 3)
                col = (1, 2, 0)[part] * D + 256 * j
                load(G_CI + n, conv_w_in[0, :, col:col + 256].rearrange("(k p) f -> p k f", p=P),
                     "p (k f) -> p k f", k=KD)
            for n in range(KD // 2):
                load(G_CO + n, conv_w_out[0, :, 256 * n:256 * n + 256].rearrange("(k p) f -> p k f", p=P),
                     "p (k f) -> p k f", k=KD)

            def expert(t):
                e = t % E
                g = 0

                def up_like(g, w, s):
                    for h in range(2):
                        slot_free(g + h, t)
                        fill(expert_slot[g + h], w[0][bass.ds(e, 1), 512 * h:512 * h + 512, 512 * s:512 * s + 512]
                             .rearrange("a (k p) f -> p (a k) f", p=P), "p (k f) -> p k f", k=4)

                def down(g, s):
                    for h in range(2):
                        r = 512 * s + 256 * h
                        slot_free(g + h, t)
                        fill(expert_slot[g + h], moe_w_down[0][bass.ds(e, 1), r:r + 256, :]
                             .rearrange("a (k p) f -> p (a k) f", p=P), "p (k f) -> p k f", k=2)

                for s in range(STEPS):
                    up_like(g, moe_w_gate, s)
                    up_like(g + 2, moe_w_up, s)
                    g += 4
                    if s >= 1:
                        down(g, s - 1)
                        g += 2
                down(g, STEPS - 1)

            expert(0)
            sp.wait_ge(route_done, 1)
            n_pass = sp.value_load(npass[0:1, 0:1], min_val=E, max_val=2 * E)
            with sp.Fori(1, n_pass) as t:
                expert(t)
            for j in range(M_LEAD // 2):
                slot_free(j, n_pass)
                sp.sem_inc(raw_full[expert_slot[j]], 16)
            for i in range(2 * TT):
                tt, h = divmod(i, 2)
                sp.wait_ge(out_ready, i + 1)
                sp.dma_start(out[0, tt * P:(tt + 1) * P, 512 * h:512 * h + 512],
                             racc[:, tt, 512 * h:512 * h + 512]).then_inc(out_done, 16)
            sp.wait_ge(out_done, 16 * 2 * TT)

        @block.gpsimd
        def _(pool):
            pool.memset(ones[:, :], 1.0).then_inc(consts, 1)
            pool.memset(ident[:, :], 0.0).then_inc(consts, 1)
            pool.memset(eps, EPS).then_inc(consts, 1)
            pool.memset(tss, 1.0).then_inc(consts, 1)
            pool.iota(iota[:, :], pattern=[[1, P]], base=0, channel_multiplier=0,
                      allow_small_or_imprecise_dtypes=True).then_inc(consts, 1)
            pool.memset(slot_of[:, :, :], -1.0).then_inc(consts, 1)
            pool.wait_ge(consts, 6)
            pool.affine_select(out=ident[:, :], in_=ident[:, :], compare_op=ALU.not_equal, fill=1.0,
                               base=0, pattern=[[-1, P]], channel_multiplier=1).then_inc(consts, 1)
            pool.affine_select(out=before[:, :], in_=ones[:, :], compare_op=ALU.is_gt, fill=0.0,
                               base=0, pattern=[[1, P]], channel_multiplier=-1).then_inc(consts, 1)
            made = [0]

            def banded(ins):
                made[0] += 1
                ins.then_inc(bands, 1)

            wide = len(WINDOWS)
            windows = WINDOWS + WINDOWS[-1:]
            for i, w in enumerate(windows):
                banded(pool.memset(band[:, i, :], 1.0 / w))
            assert WINDOWS[-1] == OLD + 2 and WINDOWS[-2] <= OLD
            pool.wait_ge(bands, made[0])
            banded(pool.memset(band[:, wide, OLD:OLD + 1], 1.0 / (OLD + 1)))
            pool.wait_ge(bands, made[0])
            banded(pool.affine_select(out=band[:, :, :], in_=band[:, :, :], compare_op=ALU.is_ge, fill=0.0, base=0,
                                      pattern=[[0, wide + 1], [1, T]], channel_multiplier=-1))
            pool.wait_ge(bands, made[0])
            for i, w in enumerate(windows):
                banded(pool.affine_select(out=band[:, i, :], in_=band[:, i, :], compare_op=ALU.is_ge, fill=0.0, base=w - 1,
                                          pattern=[[-1, T]], channel_multiplier=1))
            pool.wait_ge(bands, made[0])
            for i, w in enumerate(windows):
                banded(pool.affine_select(out=band[:, i, :], in_=band[:, i, :], compare_op=ALU.not_equal, fill=1.0 / w - 1.0,
                                          base=0, pattern=[[1, T]], channel_multiplier=-1))
            pool.wait_ge(bands, made[0])
            banded(pool.affine_select(out=band[:, wide, OLD:OLD + 1], in_=band[:, wide, OLD:OLD + 1], compare_op=ALU.not_equal,
                                      fill=1.0 / (OLD + 1) - 1.0, base=OLD, pattern=[[0, 1]], channel_multiplier=-1))
            assert made[0] == N_BANDS
            for nn in (1, 2):
                if nn == 2:
                    pool.wait_ge(ss_ready, 2)
                for c in range(1, KD):
                    pool.wait_ge(sq_done, KD * (nn - 1) + c + 1)
                    if c > 1:
                        pool.wait_ge(sum_done, (KD - 1) * (nn - 1) + c - 1)
                    pool.tensor_tensor(ssq[:, 0, :], xn[:, 0:NS] if c == 1 else ssq[:, 0, :],
                                       xn[:, c * T:c * T + NS], ALU.add).then_inc(sum_done, 1)
            pool.wait_ge(sub_done, Q_MOE)
            pool.memset(y_hi[:, :].bitcast(F32), 0.0).then_inc(arena_zero, 1)
            pool.memset(y_lo[:, :].bitcast(F32), 0.0).then_inc(arena_zero, 1)
            pool.memset(pickT[:, :, :].bitcast(F32), 0.0).then_inc(arena_zero, 1)

        @block.scalar
        def _(act):
            act.sem_inc(silu_done, 1)
            act.sem_inc(pickT_done, 1)
            def hi(q, turns=0, t=0):
                if q % 2 == 0:
                    act.wait_ge(raw_full[raw_slot(q)], loaded(q, turns, t))
                if q >= RING:
                    act.wait_ge(sub_done, q - RING + 1 + 2 * RING * turns)
                nc.scalar.activation(w_hi[:, q % RING, :],
                                     raw_sub(q), ACT.Copy).then_inc(hi_done, 1)

            def root(nn, summed, bank, n):
                act.wait_ge(ss_ready, summed)
                nc.scalar.activation(rs[:, 0, 0:n], ps[:, bank, 0:n], ACT.Sqrt, bias=eps,
                                     scale=1.0 / D).then_inc(root_done, 1)

            def residual_hi(nn, chunks=range(KD)):
                gain = (DN, CN)[nn - 1]
                for c in chunks:
                    act.wait_ge(x_new, KD * (nn - 1) + c + 1)
                    nc.scalar.activation(xn[:, c * T:c * T + NS], X[:, c, OLD:T], ACT.Square).then_inc(sq_done, 1)
                    nc.scalar.activation(n_hi[:, c, :], X[:, c, OLD:T], ACT.Copy,
                                         scale=prm[:, gain + c:gain + c + 1]).then_inc(n_hi_done, 1)

            act.wait_ge(consts, 8)
            nc.scalar.activation(warm[:, 0:1], eps, ACT.Sqrt)
            for a, rows in enumerate((P, P, T - 2 * P)):
                act.wait_ge(tok_in[a], 32 if a == 0 else 16)
                nc.scalar.activation(xn[0:rows, 0:D], tok[0:rows, a, :], ACT.Square,
                                     accum_out=tss[0:rows, a:a + 1]).then_inc(tok_squared, 1)
                act.wait_ge(tok_squared, a + 1)
            nc.scalar.activation(tss, tss, ACT.Sqrt, bias=eps, scale=1.0 / D).then_inc(tok_root, 1)
            act.wait_ge(tok_turned, 1)
            nc.scalar.activation(X[:, 0:4, 0:P], ps[:, 0, :].rearrange("p (k t) -> p k t", k=4), ACT.Copy).then_inc(x_act, 1)
            act.wait_ge(tok_inverse, 1)
            nc.scalar.activation(tok_n[:, 0, :], tok[:, 0, :], ACT.Copy, scale=tss[:, 0:1]).then_inc(tok_n_act, 1)
            act.wait_ge(tok_turned, 3)
            nc.scalar.activation(X[:, 0:4, P:2 * P], ps[:, 2, :].rearrange("p (k t) -> p k t", k=4), ACT.Copy).then_inc(x_act, 1)
            act.wait_ge(tok_turned, 5)
            nc.scalar.activation(X[:, :, 2 * P:T], ps[:, 4, 0:KD * (T - 2 * P)].rearrange("p (k t) -> p k t", k=KD),
                                 ACT.Copy).then_inc(x_act, 1)
            hi(0)
            hi(1)
            act.wait_ge(x_dve, 3)
            for c in range(KD):
                act.wait_ge(d_ready, c + 1)
                nc.scalar.activation(n_hi[:, c, :], ps[:, c, 0:NS], ACT.Copy,
                                     scale=prm[:, PN + c:PN + c + 1]).then_inc(n_hi_done, 1)
            hi(2)
            hi(3)
            residual_hi(1, range(4))
            hi(4)
            residual_hi(1, range(4, KD))
            hi(5)
            root(1, 1, 4, NS)

            sg = xn[:, 0:2 * 2 * NS].rearrange("p (b m t) -> p b m t", b=2, m=2)
            hf = xn[:, 2 * 2 * NS:4 * 2 * NS].rearrange("p (b m t) -> p b m t", b=2, m=2)

            with act.Fori(0, 2) as it:
                for n in range(STEPS):
                    q = 2 * G_GU + 4 * n + LEAD
                    hi(q, 2 * it)
                    hi(q + 1, 2 * it)
                    act.wait_ge(gate_normed, 1 + STEPS * it + n + 1)
                    b = n % 2
                    nc.scalar.activation(sg[:, b], sg[:, b], ACT.Silu).then_inc(gate_silu, 1)
                    hi(q + 2, 2 * it)
                    hi(q + 3, 2 * it)
                    act.wait_ge(dense_mul, 1 + STEPS * it + n + 1)
                    nc.scalar.activation(hid_hi[:, bass.ds(2 * STEPS * it + 2 * n, 2), :], hf[:, b], ACT.Copy).then_inc(dense_hi, 1)

            q = 2 * G_DN + LEAD
            for _ in range(2 * STEPS):
                hi(q)
                q += 1
            residual_hi(2, range(4))
            for _ in range(2 * STEPS):
                hi(q)
                q += 1
            residual_hi(2, range(4, KD))
            root(2, 3, 7, NS)

            zf = xn[:, 6 * NS:6 * NS + 2 * SEQ].rearrange("p (m t) -> p m t", m=2)
            for j in range(KD // 2):
                hi(q)
                hi(q + 1)
                for i in range(2, 6):
                    hi(q + i)
                q += 6
                act.wait_ge(z_made, j + 1)
                nc.scalar.activation(hid_hi[:, 2 * j:2 * j + 2, 0:SEQ], zf, ACT.Copy).then_inc(z_hi_done, 1)
            while q < Q_MOE:
                hi(q)
                q += 1

            def residual_out(i):
                tt, h = TURNS[i]
                act.wait_ge(racc_turned, i + 1)
                nc.scalar.activation(racc[:, tt, 512 * h:512 * h + 512], ps[:, RT_BANK[i], :],
                                     ACT.Copy).then_inc(racc_done, 1)

            for i in range(KD // 2):
                for c in (2 * i, 2 * i + 1):
                    act.wait_ge(x_new, 2 * KD + c + 1)
                    nc.scalar.activation(xn_sq[:, c, :], X[:, c, N_META:T], ACT.Square).then_inc(sq_done, 1)
                if i < M_LEAD // 2:
                    hi(q)
                    hi(q + 1)
                    q += 2
            residual_out(0)
            residual_out(1)
            act.wait_ge(ss_ready, 4)
            nc.scalar.activation(rstd, ps[:, 7, 0:TT], ACT.Sqrt, bias=eps, scale=1.0 / D).then_inc(root_done, 1)
            act.wait_ge(rstd_done, 1)
            for i, (tt, h) in enumerate(TURNS):
                act.wait_ge(hn_turned, i + 1)
                nc.scalar.activation(hn_hi[:, tt, 512 * h:512 * h + 512], ps[:, HT_BANK[i], :],
                                     ACT.Copy, scale=rstd[:, tt:tt + 1]).then_inc(hn_hi_done, 1)
            residual_out(2)
            residual_out(3)
            act.wait_ge(logit_gap, 1)
            nc.scalar.activation(gw[:, 1, :], gw[:, 0, :], ACT.Exp).then_inc(gap_exp, 1)
            nc.scalar.activation(warm[:, 0:1], eps, ACT.Silu)
            act.wait_ge(hn_turned, 2 * TT)
            act.dma_start(gfin[:, :], final_norm.rearrange("(a d) -> a d", a=1).to_broadcast([P, D])).then_inc(final_in, 16)

            def gathered(t):
                act.wait_ge(gath_ready, 3 * t + 1)
                nc.scalar.activation(xg_hi[:, :, :], ps[:, 6:8, :], ACT.Copy).then_inc(xg_hi_done, 1)

            def y_high(t):
                act.wait_ge(sub_done, Q_MOE + PASS_S * (t + 1))
                act.wait_ge(slot_gate_done, 1 + t + 1)
                for h in range(2):
                    nc.scalar.activation(y_hi[:, 512 * h:512 * h + 512], ps[:, 4 + h, :], ACT.Copy,
                                         scale=slot_gate).then_inc(y_hi_done, 1)

            gathered(0)
            act.wait_ge(route_done, 1)
            n_pass = act.value_load(npass[0:1, 0:1], min_val=E, max_val=2 * E)
            with act.Fori(0, n_pass) as t:
                turns = t * (PASS_S // (2 * RING))
                for r in range(M_LEAD, PASS_S + M_LEAD):
                    for s in range(STEPS):
                        if r == up_step(s) + 4 + BEHIND:
                            act.wait_ge(sub_done, Q_MOE + PASS_S * t + up_step(s) + 4)
                            act.wait_ge(mul_done, 1 + STEPS * t + s)
                            nc.scalar.activation(silu_m[:, :], ps[:, 0, :], ACT.Silu).then_inc(silu_done, 1)
                        if r == turn_after(s) + 1 + (BEHIND if s < STEPS - 1 else 3):
                            act.wait_ge(hid_turned, STEPS * t + s + 1)
                            nc.scalar.activation(mT_hi[:, :, :], ps[:, 2, :], ACT.Copy).then_inc(mT_hi_done, 1)
                    if r == up_end(2) + 1 + BEHIND:
                        act.wait_ge(pickT_ready, t + 1)
                        nc.scalar.activation(pickT[:, :, :], ps[:, 3, 0:TT * P], ACT.Copy).then_inc(pickT_done, 1)
                    if r == PASS_S + 1:
                        gathered(t + 1)
                    hi(Q_MOE + r, turns, t)
                y_high(t)
            nc.scalar.activation(warm[:, 1:2], eps, ACT.Sqrt)
            for tt in range(TT):
                act.wait_ge(comb_added, TT * n_pass + tt + 1)
                nc.scalar.activation(junk[:, :], racc[:, tt, :], ACT.Square, accum_out=ssum[:, tt:tt + 1]).then_inc(out_squared, 1)
                act.wait_ge(out_squared, tt + 1)
                nc.scalar.activation(rstd[:, tt:tt + 1], ssum[:, tt:tt + 1], ACT.Sqrt, bias=eps,
                                     scale=1.0 / D).then_inc(out_root, 1)

        @block.vector
        def _(dve):
            dve.sem_inc(gate_normed, 1)
            dve.sem_inc(up_normed, 1)
            dve.sem_inc(dense_mul, 1)
            dve.sem_inc(dense_lo, 1)
            dve.sem_inc(mul_done, 1)
            dve.sem_inc(slot_gate_done, 1)
            dve.sem_inc(y_lo_done, 2)
            steps = [0]

            def link(ins):
                steps[0] += 1
                ins.then_inc(dve_step, 1)
                dve.wait_ge(dve_step, steps[0])

            def lo(q, turns=0):
                dve.wait_ge(hi_done, q + 1 + 2 * RING * turns)
                nc.vector.tensor_tensor(w_lo[:, q % RING, :],
                                        raw_sub(q),
                                        w_hi[:, q % RING, :].bitcast(F32), ALU.subtract).then_inc(lo_done, 1)

            def residual_lo(nn, c):
                gain = (DN, CN)[nn - 1]
                dve.wait_ge(n_hi_done, KD * nn + c + 1)
                nc.vector.scalar_tensor_tensor(out=n_lo[:, c, :], in0=X[:, c, OLD:T], scalar=prm[:, gain + c:gain + c + 1],
                                               in1=n_hi[:, c, :].bitcast(F32), op0=ALU.mult,
                                               op1=ALU.subtract).then_inc(n_lo_done, 1)

            def inverse(nn):
                dve.wait_ge(root_done, nn)
                nc.vector.reciprocal(rs[:, :, :], rs[:, :, :]).then_inc(inverse_done, 1)
                dve.wait_ge(inverse_done, nn)

            dve.wait_ge(tok_turned, 2)
            nc.vector.tensor_copy(X[:, 4:8, 0:P], ps[:, 1, :].rearrange("p (k t) -> p k t", k=4)).then_inc(x_dve, 1)
            dve.wait_ge(tok_root, 1)
            nc.vector.reciprocal(tss, tss).then_inc(tok_inverse, 1)
            dve.wait_ge(tok_inverse, 1)
            nc.vector.tensor_scalar(tok_n[:, 1, :], tok[:, 1, :], tss[:, 1:2], None, ALU.mult).then_inc(tok_n_dve, 1)
            R = T - 2 * P
            nc.vector.tensor_scalar(tok_n[0:R, 2, :], tok[0:R, 2, :], tss[0:R, 2:3], None, ALU.mult).then_inc(tok_n_dve, 1)
            dve.wait_ge(tok_turned, 4)
            nc.vector.tensor_copy(X[:, 4:8, P:2 * P], ps[:, 3, :].rearrange("p (k t) -> p k t", k=4)).then_inc(x_dve, 1)
            dve.wait_ge(tok_turned, 6)
            nc.vector.tensor_copy(prm[:, :], ps[:, 6, 0:64]).then_inc(x_dve, 1)
            dve.wait_ge(x_dve, 3)
            lo(0)
            lo(1)
            for c in range(KD):
                dve.wait_ge(n_hi_done, c + 1)
                nc.vector.scalar_tensor_tensor(out=n_lo[:, c, :], in0=ps[:, c, 0:NS], scalar=prm[:, PN + c:PN + c + 1],
                                               in1=n_hi[:, c, :].bitcast(F32), op0=ALU.mult,
                                               op1=ALU.subtract).then_inc(n_lo_done, 1)
            lo(2)
            dve.wait_ge(x_act, 3)
            for c in range(KD):
                if c == 4:
                    lo(3)
                dve.wait_ge(sub_done, c // 4 + 1)
                nc.vector.scalar_tensor_tensor(out=X[:, c, OLD:T], in0=ps[:, c, 0:NS],
                                               scalar=prm[:, PS + c:PS + c + 1], in1=X[:, c, OLD:T],
                                               op0=ALU.mult, op1=ALU.add).then_inc(x_new, 1)
                if c % 4:
                    residual_lo(1, c - 1)
                if c % 4 == 3:
                    residual_lo(1, c)
            lo(4)
            lo(5)
            inverse(1)

            sg = xn[:, 0:2 * 2 * NS].rearrange("p (b m t) -> p b m t", b=2, m=2)
            hf = xn[:, 2 * 2 * NS:4 * 2 * NS].rearrange("p (b m t) -> p b m t", b=2, m=2)
            rs_m = rs[:, :, :].to_broadcast([P, 2, NS])
            with dve.Fori(0, 2) as it:
                for n in range(STEPS):
                    q = 2 * G_GU + 4 * n + LEAD
                    b = n % 2
                    lo(q, 2 * it)
                    lo(q + 1, 2 * it)
                    dve.wait_ge(dense_lo, 1 + STEPS * it + (n - 1 if n >= 2 else 0))
                    dve.wait_ge(sub_done, 2 * G_GU + 4 * (STEPS * it + n) + 2)
                    nc.vector.tensor_tensor(sg[:, b], ps[:, 4 * b:4 * b + 2, 0:NS], rs_m, ALU.mult).then_inc(gate_normed, 1)
                    lo(q + 2, 2 * it)
                    dve.wait_ge(sub_done, 2 * G_GU + 4 * (STEPS * it + n) + 4)
                    nc.vector.tensor_tensor(hf[:, b], ps[:, 4 * b + 2:4 * b + 4, 0:NS], rs_m, ALU.mult).then_inc(up_normed, 1)
                    dve.wait_ge(gate_silu, STEPS * it + n + 1)
                    dve.wait_ge(up_normed, 1 + STEPS * it + n + 1)
                    nc.vector.tensor_tensor(hf[:, b], hf[:, b], sg[:, b], ALU.mult).then_inc(dense_mul, 1)
                    lo(q + 3, 2 * it)
                    dve.wait_ge(dense_hi, STEPS * it + n + 1)
                    at_ = bass.ds(2 * STEPS * it + 2 * n, 2)
                    nc.vector.tensor_tensor(hid_lo[:, at_, :], hf[:, b], hid_hi[:, at_, :].bitcast(F32),
                                            ALU.subtract).then_inc(dense_lo, 1)
            q = 2 * G_DN + LEAD
            for half in range(2):
                for _ in range(2 * STEPS):
                    lo(q)
                    q += 1
                for c in range(4 * half, 4 * half + 4):
                    if c % 4 < 3:
                        dve.wait_ge(down_ready, 3 * half + c % 4 + 1)
                    else:
                        dve.wait_ge(sub_done, 2 * G_DN + 2 * STEPS * (half + 1))
                    nc.vector.tensor_tensor(X[:, c, OLD:T], ps[:, (c + 4) % 8, 0:NS], X[:, c, OLD:T], ALU.add).then_inc(x_new, 1)
                for c in range(4 * half, 4 * half + 4):
                    residual_lo(2, c)
            inverse(2)
            link(nc.vector.tensor_tensor(rs2[:, :, :], rs[:, :, :], rs[:, :, :], ALU.mult))
            rs2_m = rs2[:, :, :].to_broadcast([P, 2, NS])
            rs_out = rs[:, :, TAPS - 1:NS].to_broadcast([P, 2, SEQ])
            cs = xn[:, 0:2 * NS].rearrange("p (m t) -> p m t", m=2)
            u = xn[:, 2 * NS:4 * NS].rearrange("p (m t) -> p m t", m=2)
            y = xn[:, 4 * NS:4 * NS + 2 * SEQ].rearrange("p (m t) -> p m t", m=2)
            zf = xn[:, 6 * NS:6 * NS + 2 * SEQ].rearrange("p (m t) -> p m t", m=2)
            for j in range(KD // 2):
                lo(q)
                lo(q + 1)
                if j:
                    dve.wait_ge(u_made, j)
                dve.wait_ge(sub_done, 2 * G_CI + 6 * j + 2)
                nc.vector.tensor_tensor(cs, ps[:, 0:2, 0:NS], rs2_m, ALU.mult).then_inc(c_taken, 1)
                lo(q + 2)
                lo(q + 3)
                dve.wait_ge(c_taken, j + 1)
                dve.wait_ge(sub_done, 2 * G_CI + 6 * j + 4)
                ins = nc.vector.tensor_tensor(u, cs, ps[:, 2:4, 0:NS], ALU.mult)
                ins.then_inc(u_made, 1)
                dve.wait_ge(u_made, j + 1)
                if j:
                    dve.wait_ge(z_made, j)
                for m in range(2):
                    for k in range(TAPS):
                        tap = prm[:, CK + KD * k + 2 * j + m:CK + KD * k + 2 * j + m + 1]
                        if k == 0:
                            link(nc.vector.tensor_scalar(y[:, m], u[:, m, 0:SEQ], tap, None, ALU.mult))
                        else:
                            link(nc.vector.scalar_tensor_tensor(out=y[:, m], in0=u[:, m, k:k + SEQ], scalar=tap,
                                                                in1=y[:, m], op0=ALU.mult, op1=ALU.add))
                lo(q + 4)
                lo(q + 5)
                q += 6
                link(nc.vector.tensor_tensor(y, y, rs_out, ALU.mult))
                dve.wait_ge(sub_done, 2 * G_CI + 6 * j + 6)
                if j:
                    dve.wait_ge(z_lo_done, j)
                nc.vector.tensor_tensor(zf, y, ps[:, 4:6, TAPS - 1:NS], ALU.mult).then_inc(z_made, 1)
                dve.wait_ge(z_hi_done, j + 1)
                nc.vector.tensor_tensor(hid_lo[:, 2 * j:2 * j + 2, 0:SEQ], zf,
                                        hid_hi[:, 2 * j:2 * j + 2, 0:SEQ].bitcast(F32), ALU.subtract).then_inc(z_lo_done, 1)
            while q < Q_MOE:
                lo(q)
                q += 1
            for c in range(KD):
                if c % 2 == 0:
                    dve.wait_ge(conv_ready, c // 2 + 1)
                else:
                    dve.wait_ge(sub_done, 2 * G_CO + c + 1)
                nc.vector.tensor_tensor(X[:, c, N_META:T], ps[:, (c + 6) % 8, 0:SEQ], X[:, c, N_META:T],
                                        ALU.add).then_inc(x_new, 1)
                dve.wait_ge(x_new, 2 * KD + c + 1)
                nc.vector.tensor_scalar(xg32[:, c, :], X[:, c, N_META:T], prm[:, MN + c:MN + c + 1], None,
                                        ALU.mult).then_inc(xg32_done, 1)
                if c % 2 and c < M_LEAD:
                    lo(Q_MOE + c - 1)
                    lo(Q_MOE + c)

            dve.wait_ge(consts, 8)
            dve.wait_ge(root_done, 3)
            nc.vector.reciprocal(rstd, rstd).then_inc(rstd_done, 1)
            dve.wait_ge(rstd_done, 1)
            dve.wait_ge(lg_ready, 1)
            link(nc.vector.tensor_copy(lg[:, :, :], ps[:, 6, 0:TT * E].rearrange("p (a e) -> p a e", a=TT)))
            for tt in range(TT):
                ins = nc.vector.max(mx[:, tt, :], lg[:, tt, :])
            link(ins)
            for tt in range(TT):
                ins = nc.vector.max_index(ix[:, tt, :], mx[:, tt, :], lg[:, tt, :])
            link(ins)
            link(nc.vector.tensor_copy(ixf[:, :, :], ix[:, :, :]))
            for tt in range(TT):
                nc.vector.tensor_scalar(oh1[:, tt, :], iota[:, 0:E], ixf[:, tt, 0:1], None, ALU.is_equal)
                link(nc.vector.tensor_scalar(oh2[:, tt, :], iota[:, 0:E], ixf[:, tt, 1:2], None, ALU.is_equal))
            nc.vector.tensor_tensor(mask[:, :, :], oh1[:, :, :], oh2[:, :, :], ALU.add).then_inc(mask_done, 1)
            link(nc.vector.tensor_tensor(gw[:, 0, :], mx[:, :, 1], mx[:, :, 0], ALU.subtract))
            nc.vector.tensor_tensor(gw[:, 0, :], gw[:, 0, :], rstd, ALU.mult).then_inc(logit_gap, 1)

            def normed_lo(i):
                tt, h = TURNS[i]
                at_ = slice(512 * h, 512 * h + 512)
                dve.wait_ge(hn_hi_done, i + 1)
                nc.vector.scalar_tensor_tensor(out=hn_lo[:, tt, at_], in0=ps[:, HT_BANK[i], :],
                                               scalar=rstd[:, tt:tt + 1], in1=hn_hi[:, tt, at_].bitcast(F32),
                                               op0=ALU.mult, op1=ALU.subtract).then_inc(hn_lo_done, 1)

            normed_lo(0)
            dve.wait_ge(mask_done, 1)
            dve.wait_ge(pos_ready, 1)
            link(nc.vector.scalar_tensor_tensor(out=rank[:, :, :], in0=ps[:, 6, 32:32 + TT * E].rearrange("p (a e) -> p a e", a=TT),
                                                scalar=1.0, in1=mask[:, :, :], op0=ALU.add, op1=ALU.mult))
            nc.vector.tensor_scalar(slot_of[:, :, E:2 * E], rank[:, :, :], -1.0 - P, None, ALU.add)
            link(nc.vector.tensor_scalar(slot_of[:, :, 0:E], rank[:, :, :], -1.0, None, ALU.add))

            def make_pick(t):
                for tt in range(TT):
                    ins = nc.vector.tensor_scalar(pick[:, tt, :], iota[:, :], slot_of[:, tt, bass.ds(t, 1)], None,
                                                  ALU.is_equal)
                ins.then_inc(pick_done, 1)

            make_pick(0)
            dve.wait_ge(count_ready, 1)
            link(nc.vector.tensor_reduce(cmax, ps[:, 7, 0:E], AX_X, ALU.max))
            link(nc.vector.tensor_scalar(cmax, cmax, float(P), float(E), ALU.is_gt, ALU.mult))
            nc.vector.tensor_scalar(npass[:, :], cmax, float(E), None, ALU.add).then_inc(route_done, 1)
            for i in range(1, 2 * TT):
                normed_lo(i)
            dve.wait_ge(gap_exp, 1)
            link(nc.vector.tensor_scalar(gw[:, 2, :], gw[:, 1, :], 1.0, None, ALU.add))
            link(nc.vector.reciprocal(gw[:, 2, :], gw[:, 2, :]))
            link(nc.vector.tensor_tensor(gw[:, 3, :], gw[:, 1, :], gw[:, 2, :], ALU.mult))
            for tt in range(TT):
                link(nc.vector.tensor_scalar(gates[:, tt, :], oh1[:, tt, :], gw[:, 2, tt:tt + 1], None, ALU.mult))
                nc.vector.scalar_tensor_tensor(out=gates[:, tt, :], in0=oh2[:, tt, :], scalar=gw[:, 3, tt:tt + 1],
                                               in1=gates[:, tt, :], op0=ALU.mult, op1=ALU.add).then_inc(gates_done, 1)

            def gathered(t):
                for h, bank in enumerate((0, 3)):
                    dve.wait_ge(gath_ready, 3 * t + 2 + h)
                    nc.vector.tensor_copy(xg_lo[:, 4 * h:4 * h + 4, :],
                                          ps[:, bank, :].rearrange("p (k t) -> p k t", k=4)).then_inc(xg_lo_done, 1)

            def y_low(t):
                for h in range(2):
                    at_ = slice(512 * h, 512 * h + 512)
                    dve.wait_ge(y_hi_done, 2 * t + h + 1)
                    nc.vector.scalar_tensor_tensor(out=y_lo[:, at_], in0=ps[:, 4 + h, :], scalar=slot_gate,
                                                   in1=y_hi[:, at_].bitcast(F32), op0=ALU.mult,
                                                   op1=ALU.subtract).then_inc(y_lo_done, 1)

            def combined(t):
                for h in range(2):
                    at_ = slice(512 * h, 512 * h + 512)
                    for tt in range(TT):
                        dve.wait_ge(comb_ready, 2 * TT * t + TT * h + tt + 1)
                        ins = nc.vector.tensor_tensor(racc[:, tt, at_], ps[:, (6, 2)[tt] + h, :], racc[:, tt, at_], ALU.add)
                        if h == 1:
                            ins.then_inc(comb_added, 1)

            gathered(0)
            dve.wait_ge(route_done, 1)
            n_pass = dve.value_load(npass[0:1, 0:1], min_val=E, max_val=2 * E)
            with dve.Fori(0, n_pass) as t:
                turns = t * (PASS_S // (2 * RING))
                for r in range(M_LEAD, PASS_S + M_LEAD):
                    if r == 11:
                        combined(t)
                    for s in range(STEPS):
                        if r == up_end(s) + BEHIND:
                            dve.wait_ge(silu_done, 1 + STEPS * t + s + 1)
                            dve.wait_ge(sub_done, Q_MOE + PASS_S * t + up_end(s) + 1)
                            nc.vector.tensor_tensor(hid_m[:, :], silu_m[:, :], ps[:, 1, :], ALU.mult).then_inc(mul_done, 1)
                        if r == turn_after(s) + (BEHIND if s < STEPS - 1 else 3):
                            dve.wait_ge(mT_hi_done, STEPS * t + s + 1)
                            nc.vector.tensor_tensor(mT_lo[:, :, :], ps[:, 2, :].rearrange("p (k t) -> p k t", k=4),
                                                    mT_hi[:, :, :].bitcast(F32), ALU.subtract).then_inc(mT_lo_done, 1)
                    if r == up_end(2) + BEHIND:
                        dve.wait_ge(pickT_done, 1 + t + 1)
                        nc.vector.tensor_copy(slot_gate, ps[:, 3, TT * P:TT * P + 1]).then_inc(slot_gate_done, 1)
                        make_pick(t + 1)
                    if r == PASS_S + 0:
                        gathered(t + 1)
                    lo(Q_MOE + r, turns)
                y_low(t)
            combined(n_pass)
            dve.wait_ge(final_in, 16)
            for tt in range(TT):
                dve.wait_ge(out_root, tt + 1)
                link(nc.vector.reciprocal(rstd[:, tt:tt + 1], rstd[:, tt:tt + 1]))
                for h in range(2):
                    at_ = slice(512 * h, 512 * h + 512)
                    nc.vector.scalar_tensor_tensor(out=racc[:, tt, at_], in0=racc[:, tt, at_], scalar=rstd[:, tt:tt + 1],
                                                   in1=gfin[:, at_], op0=ALU.mult, op1=ALU.mult).then_inc(out_ready, 1)

        @block.tensor
        def _(pe):
            mm = nc.tensor.matmul

            def use(q, turns=0):
                pe.wait_ge(lo_done, q + 1 + 2 * RING * turns)

            def features(bank, n, sub_col, q, mov_hi, mov_lo, first, last):
                wh = w_hi[:, q % RING, sub_col:sub_col + P]
                wl = w_lo[:, q % RING, sub_col:sub_col + P]
                mm(ps[:, bank, 0:n], wh, mov_hi, start=first, stop=False)
                mm(ps[:, bank, 0:n], wh, mov_lo, start=False, stop=False)
                return mm(ps[:, bank, 0:n], wl, mov_hi, start=False, stop=last)

            def mean_square(nn, bank):
                pe.wait_ge(sum_done, (KD - 1) * nn)
                mm(ps[:, bank, 0:NS], ones[:, :], ssq[:, 0, :], start=True, stop=True).then_inc(ss_ready, 1)

            pe.wait_ge(consts, 8)
            for a in range(2):
                pe.wait_ge(tok_in[a], 32 if a == 0 else 16)
                for h in range(2):
                    for k in range(4):
                        c = 4 * h + k
                        last = nc.tensor.transpose(ps[:, 2 * a + h, k * P:(k + 1) * P], tok[:, a, c * P:(c + 1) * P], ident[:, :])
                    last.then_inc(tok_turned, 1)
            R = T - 2 * P
            pe.wait_ge(tok_in[2], 16)
            for c in range(KD):
                last = nc.tensor.transpose(ps[:, 4, c * R:(c + 1) * R], tok[0:R, 2, c * P:(c + 1) * P], ident[0:R, 0:R])
            last.then_inc(tok_turned, 1)
            pe.wait_ge(param_in, 16 * 6)
            nc.tensor.transpose(ps[:, 6, 0:64], param_rows[:, :], ident[0:64, 0:64]).then_inc(tok_turned, 1)
            X_BANKS = {0: (x_act, 1), 1: (x_dve, 1), 2: (x_act, 2), 3: (x_dve, 2), 4: (x_act, 3), 6: (x_dve, 3)}
            pe.wait_ge(tok_n_act, 1)
            pe.wait_ge(tok_n_dve, 2)
            pe.wait_ge(bands, N_BANDS)
            for c in range(KD):
                if c in X_BANKS:
                    pe.wait_ge(*X_BANKS[c])
                g = c * P // GW
                f = slice(c * P, (c + 1) * P)
                mm(ps[:, c, 0:NS], tok_n[:, 0, f], band[:, g + (g == len(WINDOWS) - 1), OLD:T], start=True, stop=False)
                mm(ps[:, c, P - OLD:NS], tok_n[:, 1, f], band[:, g, 0:T - P], start=False, stop=False)
                mm(ps[:, c, 2 * P - OLD:NS], tok_n[0:R, 2, f], band[0:R, g, 0:R], start=False, stop=True).then_inc(d_ready, 1)

            for g in range(GROUPS):
                q = g // 2
                use(q)
                for m in range(2):
                    for k in range(2):
                        c = 2 * g + k
                        pe.wait_ge(n_lo_done, 2 * g + 2)
                        last = features(2 * g + m, NS, (g % 2) * 2 * GW + k * GW + m * P, q,
                                        n_hi[:, c, :], n_lo[:, c, :], k == 0, k == 1)
                if g % 2:
                    last.then_inc(sub_done, 1)

            with pe.Fori(0, 2) as it:
                for n in range(STEPS):
                    q = 2 * G_GU + 4 * n
                    b = 4 * (n % 2)
                    if n == 1:
                        pe.wait_ge(root_done, 1)
                    for part in range(2):
                        pe.wait_ge((gate_normed, up_normed)[part], 1 + STEPS * it + (n - 1 if n >= 2 else 0))
                        if n == 0 and part == 1:
                            mean_square(1, 4)
                        for s in range(2):
                            use(q, 2 * it)
                            for m in range(2):
                                for k in range(4):
                                    c = 4 * s + k
                                    if n == 0 and part == 0:
                                        pe.wait_ge(n_lo_done, KD + c + 1)
                                    last = features(b + 2 * part + m, NS, k * 256 + m * P, q, n_hi[:, c, :], n_lo[:, c, :],
                                                    c == 0, c == KD - 1)
                            last.then_inc(sub_done, 1)
                            q += 1
            q = 2 * G_DN
            for half in range(2):
                pe.wait_ge(dense_mul, 1 + 2 * STEPS - 1 + half)
                for i in range(2 * STEPS):
                    use(q)
                    if half == 0:
                        pe.wait_ge(dense_lo, 1 + i + 1)
                    for c in range(4):
                        for k in range(2):
                            f = 2 * i + k
                            last = features((4 * half + c + 4) % 8, NS, k * 512 + c * P, q, hid_hi[:, f, :], hid_lo[:, f, :],
                                            f == 0, f == KF - 1)
                        if i == 2 * STEPS - 1 and c < 3:
                            last.then_inc(down_ready, 1)
                    last.then_inc(sub_done, 1)
                    q += 1
            for j in range(KD // 2):
                for part in range(3):
                    for s in range(2):
                        use(q)
                        if j and s == 0:
                            pe.wait_ge((c_taken, u_made, z_made)[part], j)
                        for m in range(2):
                            if j == 0 and part == 0 and s == 0:
                                pe.wait_ge(x_new, KD + 4 + m + 1)
                            for k in range(4):
                                c = 4 * s + k
                                if j == 0 and part == 0 and m == 0:
                                    pe.wait_ge(n_lo_done, 2 * KD + c + 1)
                                last = features(2 * part + m, NS, k * 256 + m * P, q, n_hi[:, c, :], n_lo[:, c, :],
                                                c == 0, c == KD - 1)
                        last.then_inc(sub_done, 1)
                        q += 1
                    if j == 0 and part == 0:
                        mean_square(2, 7)
            def statistics(pair):
                for c in (2 * pair, 2 * pair + 1):
                    pe.wait_ge(sq_done, 2 * KD + max(c, 1) + 1)
                    for tt in range(TT):
                        last = mm(ps[:, 7, tt:tt + 1], xn_sq[:, c, tt * P:(tt + 1) * P], ones[:, 0:1],
                                  start=(c == 0 and tt == 0), stop=(c == KD - 1), skip_group_check=True)
                if pair == KD // 2 - 1:
                    last.then_inc(ss_ready, 1)
                for c in (2 * pair, 2 * pair + 1):
                    pe.wait_ge(xg32_done, c + 1)
                    for tt in range(TT):
                        last = mm(ps[:, 6, tt * E:(tt + 1) * E], xg32[:, c, tt * P:(tt + 1) * P], r32[:, c, :],
                                  start=(c == 0 and tt == 0), stop=(c == KD - 1), skip_group_check=True)
                if pair == KD // 2 - 1:
                    last.then_inc(lg_ready, 1)

            def turn(src, first, i, banks, ready):
                tt, h = TURNS[i]
                for k in range(4):
                    col = first + tt * P
                    last = nc.tensor.transpose(ps[:, banks[i], k * P:(k + 1) * P], src[:, 4 * h + k, col:col + P], ident[:, :])
                last.then_inc(ready, 1)

            for i in range(KD // 2):
                if i == 1:
                    pe.wait_ge(z_made, KD // 2)
                for s in range(2):
                    use(q)
                    for m in range(2):
                        for k in range(4):
                            c = 4 * s + k
                            if i == 0 and m == 0:
                                pe.wait_ge(z_lo_done, c // 2 + 1)
                            last = features((2 * i + m + 6) % 8, SEQ, k * 256 + m * P, q, hid_hi[:, c, 0:SEQ],
                                            hid_lo[:, c, 0:SEQ], c == 0, c == KD - 1)
                        if s == 1 and m == 0:
                            last.then_inc(conv_ready, 1)
                    last.then_inc(sub_done, 1)
                    q += 1
                    if i and s == (i < 3):
                        if i == 1:
                            pe.wait_ge(router_in, 16)
                        statistics(i - 1)
                        if i == 2:
                            turn(X, N_META, 0, RT_BANK, racc_turned)
                            turn(X, N_META, 1, RT_BANK, racc_turned)
            for i in range(2 * TT):
                if i == 2:
                    statistics(KD // 2 - 1)
                if i >= 2:
                    pe.wait_ge(racc_done, i - 1)
                turn(xg32, 0, i, HT_BANK, hn_turned)
            turn(X, N_META, 2, RT_BANK, racc_turned)
            turn(X, N_META, 3, RT_BANK, racc_turned)
            pe.wait_ge(mask_done, 1)
            for tt in range(TT):
                o = ps[:, 6, 32 + tt * E:32 + (tt + 1) * E]
                for s in range(tt):
                    mm(o, ones[:, :], mask[:, s, :], start=(s == 0), stop=False)
                last = mm(o, before[:, :], mask[:, tt, :], start=(tt == 0), stop=True)
            last.then_inc(pos_ready, 1)
            for tt in range(TT):
                last = mm(ps[:, 7, 0:E], ones[:, :], mask[:, tt, :], start=(tt == 0), stop=(tt == TT - 1))
            last.then_inc(count_ready, 1)
            def gather(src, banks):
                for c in range(KD):
                    if src is hn_hi and c == KD // 2:
                        pe.wait_ge(route_done, 1)
                    for tt in range(TT):
                        last = mm(ps[:, banks[c // 4], (c % 4) * P:(c % 4 + 1) * P], src[:, tt, c * P:(c + 1) * P],
                                  pick[:, tt, :], start=(tt == 0), stop=(tt == TT - 1))
                    if c == KD - 1 or (src is hn_lo and c == KD // 2 - 1):
                        last.then_inc(gath_ready, 1)

            def gather_hi():
                gather(hn_hi, (6, 7))

            def gather_lo():
                gather(hn_lo, (0, 3))

            def combine(t):
                pe.wait_ge(pickT_done, 1 + t)
                for h in range(2):
                    pe.wait_ge(y_lo_done, 2 * t + h + 1)
                    for tt in range(TT):
                        o = ps[:, (6, 2)[tt] + h, :]
                        mm(o, pickT[:, tt, :], y_hi[:, 512 * h:512 * h + 512], start=True, stop=False)
                        last = mm(o, pickT[:, tt, :], y_lo[:, 512 * h:512 * h + 512], start=False, stop=True)
                        last.then_inc(comb_ready, 1)

            def stream(bank, q, turns, piece, k, tok_hi, tok_lo, first, last_one):
                o = ps[:, bank, :]
                wh = w_hi[:, q % RING, piece * 512:piece * 512 + 512]
                wl = w_lo[:, q % RING, piece * 512:piece * 512 + 512]
                mm(o, tok_hi, wh, start=first, stop=False)
                mm(o, tok_hi, wl, start=False, stop=False)
                return mm(o, tok_lo, wh, start=False, stop=last_one)

            pe.wait_ge(pick_done, 1)
            pe.wait_ge(hn_hi_done, 2 * TT)
            gather_hi()
            pe.wait_ge(hn_lo_done, 2 * TT)
            gather_lo()
            pe.wait_ge(arena_zero, 3)
            pe.wait_ge(racc_done, 4)
            n_pass = pe.value_load(npass[0:1, 0:1], min_val=E, max_val=2 * E)
            with pe.Fori(0, n_pass) as t:
                turns = t * (PASS_S // (2 * RING))
                r = 0

                def up_like(bank):
                    nonlocal r
                    for i in range(4):
                        q = Q_MOE + r
                        use(q, turns)
                        if r == 2:
                            pe.wait_ge(xg_lo_done, 2 * t + 2)
                        for k in range(2):
                            c = 2 * i + k
                            last = stream(bank, q, turns, k, k, xg_hi[:, c, :], xg_lo[:, c, :], c == 0, c == KD - 1)
                        last.then_inc(sub_done, 1)
                        r += 1

                def turn_hidden(s):
                    pe.wait_ge(mul_done, 1 + STEPS * t + s + 1)
                    if s == 0:
                        pe.wait_ge(comb_added, TT * t + TT)
                    for k in range(4):
                        last = nc.tensor.transpose(ps[:, 2, k * P:(k + 1) * P], hid_m[:, k * P:(k + 1) * P], ident[:, :])
                    last.then_inc(hid_turned, 1)

                def down(s):
                    nonlocal r
                    pe.wait_ge(mT_lo_done, STEPS * t + s + 1)
                    for k in range(4):
                        q = Q_MOE + r
                        use(q, turns)
                        for h in range(2):
                            last = stream(4 + h, q, turns, h, k, mT_hi[:, k, :], mT_lo[:, k, :], s == 0 and k == 0,
                                          s == STEPS - 1 and k == 3)
                        last.then_inc(sub_done, 1)
                        r += 1

                for s in range(STEPS):
                    if s == 0:
                        pe.wait_ge(xg_hi_done, t + 1)
                        pe.wait_ge(xg_lo_done, 2 * t + 1)
                    pe.wait_ge(silu_done, 1 + STEPS * t + s)
                    up_like(0)
                    if s >= 1:
                        turn_hidden(s - 1)
                    pe.wait_ge(mul_done, 1 + STEPS * t + s)
                    up_like(1)
                    if s == 0:
                        combine(t)
                    if s == 2:
                        pe.wait_ge(comb_added, TT * t + TT)
                        pe.wait_ge(gates_done, TT)
                        for tt in range(TT):
                            nc.tensor.transpose(ps[:, 3, tt * P:(tt + 1) * P], pick[:, tt, :].bitcast(F32), ident[:, :])
                        for tt in range(TT):
                            last = mm(ps[:, 3, TT * P:TT * P + 1], pick[:, tt, :].bitcast(F32),
                                      gates[:, tt, bass.ds(t % E, 1)], start=(tt == 0), stop=(tt == TT - 1))
                        last.then_inc(pickT_ready, 1)
                    if s == STEPS - 1:
                        pe.wait_ge(pick_done, t + 2)
                        gather_hi()
                    if s >= 1:
                        down(s - 1)
                turn_hidden(STEPS - 1)
                pe.wait_ge(pickT_done, 1 + t + 1)
                pe.wait_ge(slot_gate_done, 1 + t + 1)
                pe.wait_ge(silu_done, 1 + STEPS * t + STEPS)
                gather_lo()
                down(STEPS - 1)
            combine(n_pass)


_INS = ["x", "meta_tokens", "pool_norm", "pool_w", "pool_scale", "dense_norm", "dense_w_gate", "dense_w_up",
        "dense_w_down", "conv_norm", "conv_w_in", "conv_kernel", "conv_w_out", "moe_norm", "moe_router",
        "moe_w_gate", "moe_w_up", "moe_w_down", "final_norm"]


def kernel(**inputs):
    import numpy as np
    import concourse.bacc as bacc
    from concourse import mybir as mb
    from concourse.bass_utils import run_bass_kernel_spmd

    nc = bacc.Bacc("TRN2", target_bir_lowering=False, num_devices=1)
    arrays, args = {}, []
    for name in _INS:
        a = np.ascontiguousarray(inputs[name])
        arrays[name] = a
        args.append(nc.dram_tensor(name, a.shape, mb.dt.from_np(a.dtype), kind="ExternalInput").ap())
    o = nc.dram_tensor("out", arrays["x"].shape, mb.dt.from_np(arrays["x"].dtype), kind="ExternalOutput").ap()
    build_encoder(nc, *args, o)
    r = run_bass_kernel_spmd(nc, [arrays], core_ids=[0])
    return r.results[0]["out"]
```
